# Optimizing a Trainium2 kernel written in Bass

```python
import numpy as np
import jax, jax.numpy as jnp
from jax import lax

D_MODEL = 1024
BATCH = 1
SEQ = 512
DEPTH = 2

GRID_W = 64
CTX_LEN = 256
N_MOD = 9
D_FF = (11 * D_MODEL) // 4
RMS_EPS = 1e-6
POOL_WINDOWS = (2, 4, 8, 16)
N_POOL_GROUPS = 4
POOL_W = D_MODEL // 2
POOL_GW = POOL_W // N_POOL_GROUPS
NA_HEAD_DIM = 64
NA_W = D_MODEL // 2
NA_HEADS = NA_W // NA_HEAD_DIM
NA_SCALE = NA_HEAD_DIM ** -0.5
NB_ROWS = 8
NB_COLS = 16
K_COLS = 2 * NB_COLS
D_RNN = (5 * D_MODEL) // 4
RG_BW = 128
RG_BLOCKS = D_RNN // RG_BW
CONV_W = 4
RG_C = 8.0
N_EVEN = (DEPTH + 1) // 2
N_ODD = DEPTH // 2

kernel_name = "hybrid_pool_natten_rglru_dit_block"

F32 = jnp.float32

def rms_norm(x, g):
    xf = x.astype(F32)
    y = xf * lax.rsqrt(jnp.mean(xf * xf, axis=-1, keepdims=True) + RMS_EPS)
    return y.astype(x.dtype) * g

def modulate(h, shift, scale):
    return h * (1.0 + scale) + shift

def swiglu(h, w_gu, w_down):
    u = h @ w_gu
    return (jax.nn.silu(u[..., :D_FF]) * u[..., D_FF:]) @ w_down

def heads(t):
    return t.reshape(t.shape[0], t.shape[1], NA_HEADS, NA_HEAD_DIM)

def multiscale_pool(u, pool_w, pool_scale):
    B, T, _ = u.shape
    uf = u.astype(F32).reshape(B, T, N_POOL_GROUPS, POOL_GW)
    csum = jnp.pad(jnp.cumsum(uf, axis=1), ((0, 0), (1, 0), (0, 0), (0, 0)))
    t = np.arange(T)[:, None]
    win = np.array(POOL_WINDOWS)[None, :]
    lo = np.clip(t - win // 2, 0, T)
    hi = np.clip(t + win // 2, 0, T)
    gidx = np.arange(N_POOL_GROUPS)
    wsum = csum[:, hi, gidx] - csum[:, lo, gidx]
    cnt = (hi - lo).astype(np.float32)[None, :, :, None]
    y = (wsum / cnt - uf).astype(u.dtype)
    y = jnp.einsum('btgk,gkj->btgj', y, pool_w).reshape(B, T, POOL_W)
    return y * pool_scale

def neighbourhood_attention(q, k, v, kc, vc, rpb):
    B, S, H, Dh = q.shape
    rows = S // GRID_W
    kh = min(NB_ROWS, rows)
    n_cb = GRID_W // NB_COLS
    qg = q.reshape(B, rows, GRID_W, H, Dh)
    kg = k.reshape(B, rows, GRID_W, H, Dh)
    vg = v.reshape(B, rows, GRID_W, H, Dh)
    qcols = np.arange(GRID_W).reshape(n_cb, NB_COLS)
    qstart = np.clip(qcols - NB_COLS // 2, 0, GRID_W - NB_COLS)
    slab_start = np.clip(np.arange(n_cb) * NB_COLS - NB_COLS // 2, 0, GRID_W - K_COLS)
    slab_cols = slab_start[:, None] + np.arange(K_COLS)[None, :]
    col_mask = ((slab_cols[:, None, :] >= qstart[:, :, None])
                & (slab_cols[:, None, :] < qstart[:, :, None] + NB_COLS))
    dc_idx = np.clip(slab_cols[:, None, :] - qcols[:, :, None] + NB_COLS - 1, 0, 2 * NB_COLS - 2)
    rpb_cols = rpb[:, :, dc_idx]
    mask6 = col_mask[None, None, :, :, None, :]
    n_loc = kh * K_COLS

    def row_fn(args):
        r, q_row = args
        r0 = jnp.clip(r - kh // 2, 0, rows - kh)
        k_rows = lax.dynamic_slice_in_dim(kg, r0, kh, axis=1)
        v_rows = lax.dynamic_slice_in_dim(vg, r0, kh, axis=1)
        k_slab = k_rows[:, :, slab_cols]
        v_slab = v_rows[:, :, slab_cols]
        qb = q_row.reshape(B, n_cb, NB_COLS, H, Dh)
        s_loc = jnp.einsum('bjqhd,bkjchd->bhjqkc', qb, k_slab, preferred_element_type=F32) * NA_SCALE
        dr = r0 + jnp.arange(kh) - r + (NB_ROWS - 1)
        bias = jnp.transpose(rpb_cols[:, dr], (0, 2, 3, 1, 4)).astype(F32)
        s_loc = jnp.where(mask6, s_loc + bias[None], -jnp.inf)
        s_ctx = jnp.einsum('bjqhd,bmhd->bhjqm', qb, kc, preferred_element_type=F32) * NA_SCALE
        s = jnp.concatenate([s_loc.reshape(B, H, n_cb, NB_COLS, n_loc), s_ctx], axis=-1)
        p = jax.nn.softmax(s, axis=-1).astype(v.dtype)
        p_loc = p[..., :n_loc].reshape(B, H, n_cb, NB_COLS, kh, K_COLS)
        o = (jnp.einsum('bhjqkc,bkjchd->bjqhd', p_loc, v_slab)
             + jnp.einsum('bhjqm,bmhd->bjqhd', p[..., n_loc:], vc))
        return o.reshape(B, GRID_W, H, Dh)

    out = lax.map(row_fn, (jnp.arange(rows), jnp.moveaxis(qg, 1, 0)))
    return jnp.moveaxis(out, 0, 1).reshape(B, S, H * Dh)

def context_attention(q, k, v):
    B, T = q.shape[0], q.shape[1]
    s = jnp.einsum('bqhd,bkhd->bhqk', q, k, preferred_element_type=F32) * NA_SCALE
    p = jax.nn.softmax(s, axis=-1).astype(v.dtype)
    return jnp.einsum('bhqk,bkhd->bqhd', p, v).reshape(B, T, NA_W)

def pool_nat_mixer(hx, hc, w_in, w_out, pool_w, pool_scale, rpb, need_ctx_out):
    B, S, _ = hx.shape
    ux = hx @ w_in
    px = ux[..., :POOL_W]
    qx = heads(ux[..., POOL_W:POOL_W + NA_W])
    kx = heads(ux[..., POOL_W + NA_W:POOL_W + 2 * NA_W])
    vx = heads(ux[..., POOL_W + 2 * NA_W:])
    kvc = hc @ w_in[:, POOL_W + NA_W:]
    kc = heads(kvc[..., :NA_W])
    vc = heads(kvc[..., NA_W:])
    a_x = multiscale_pool(px, pool_w, pool_scale)
    b_x = neighbourhood_attention(qx, kx, vx, kc, vc, rpb)
    yx = jnp.concatenate([a_x, b_x], axis=-1) @ w_out
    yc = None
    if need_ctx_out:
        uc = hc @ w_in[:, :POOL_W + NA_W]
        a_c = multiscale_pool(uc[..., :POOL_W], pool_w, pool_scale)
        b_c = context_attention(heads(uc[..., POOL_W:]), kc, vc)
        yc = jnp.concatenate([a_c, b_c], axis=-1) @ w_out
    return yx, yc

def centred_dwconv(u, w, b):
    T = u.shape[1]
    left = CONV_W // 2
    up = jnp.pad(u, ((0, 0), (left, CONV_W - 1 - left), (0, 0)))
    y = b
    for k in range(CONV_W):
        y = y + up[:, k:k + T] * w[k]
    return y

def rglru_coeffs(u, gate_w, gate_b, lam):
    B, T, _ = u.shape
    ub = u.reshape(B, T, RG_BLOCKS, RG_BW)
    g = jnp.einsum('btnk,gnkj->gbtnj', ub, gate_w).reshape(2, B, T, D_RNN)
    g = jax.nn.sigmoid(g.astype(F32) + gate_b.astype(F32)[:, None, None, :])
    r, i = g[0], g[1]
    log_a = -RG_C * r * jax.nn.softplus(-lam.astype(F32))
    a = jnp.exp(log_a)
    b = jnp.sqrt(-jnp.expm1(2.0 * log_a)) * (i * u.astype(F32))
    return a, b

def linear_scan(a, b, h0):
    def combine(e1, e2):
        a1, b1 = e1
        a2, b2 = e2
        return a1 * a2, a2 * b1 + b2
    a_cum, b_cum = lax.associative_scan(combine, (a, b), axis=1)
    return a_cum * h0[:, None] + b_cum

def rglru_mixer(hx, hc, w_in, conv_w, conv_b, gate_w, gate_b, lam, w_out, need_ctx_out):
    ux = hx @ w_in
    gx, rx = ux[..., :D_RNN], ux[..., D_RNN:]
    if need_ctx_out:
        uc = hc @ w_in
        gc, rc = uc[..., :D_RNN], uc[..., D_RNN:]
    else:
        rc = hc @ w_in[:, D_RNN:]
    rx = centred_dwconv(rx, conv_w, conv_b)
    rc = centred_dwconv(rc, conv_w, conv_b)
    hs_x, hs_c = [], []
    for d in range(2):
        ac, bc = rglru_coeffs(rc, gate_w[d], gate_b[d], lam[d])
        ax, bx = rglru_coeffs(rx, gate_w[d], gate_b[d], lam[d])
        if d == 1:
            ac, bc, ax, bx = (jnp.flip(t, axis=1) for t in (ac, bc, ax, bx))
        h_c = linear_scan(ac, bc, jnp.zeros_like(bc[:, 0]))
        h_x = linear_scan(ax, bx, h_c[:, -1])
        if d == 1:
            h_c, h_x = jnp.flip(h_c, axis=1), jnp.flip(h_x, axis=1)
        hs_x.append(h_x)
        hs_c.append(h_c)
    yx = (jax.nn.gelu(gx) * (hs_x[0] + hs_x[1]).astype(gx.dtype)) @ w_out
    yc = None
    if need_ctx_out:
        yc = (jax.nn.gelu(gc) * (hs_c[0] + hs_c[1]).astype(gc.dtype)) @ w_out
    return yx, yc

def setup_inputs(seed: int = 0) -> dict:
    key = jax.random.key(seed)
    ks = jax.random.split(key, 24)

    def nrm(k, shape, scale):
        return jax.random.normal(k, shape, F32) * scale

    a_c = jax.random.uniform(ks[19], (N_ODD, 2, D_RNN), F32, 0.9, 0.999)
    a_base = a_c ** (1.0 / RG_C)
    return {
        "x": nrm(ks[0], (BATCH, SEQ, D_MODEL), 1.0),
        "c": nrm(ks[1], (BATCH, D_MODEL), 1.0),
        "ctx": nrm(ks[2], (BATCH, CTX_LEN, D_MODEL), 1.0),
        "c_ctx": nrm(ks[3], (D_MODEL,), 1.0),
        "ada_w": nrm(ks[4], (DEPTH, D_MODEL, N_MOD * D_MODEL), 0.5 * D_MODEL ** -0.5),
        "ada_b": nrm(ks[5], (DEPTH, N_MOD * D_MODEL), 0.01),
        "norm_g": 1.0 + nrm(ks[6], (DEPTH, 3, D_MODEL), 0.02),
        "ffn_w_gu": nrm(ks[7], (DEPTH, 2, D_MODEL, 2 * D_FF), D_MODEL ** -0.5),
        "ffn_w_down": nrm(ks[8], (DEPTH, 2, D_FF, D_MODEL), D_FF ** -0.5),
        "ab_w_in": nrm(ks[9], (N_EVEN, D_MODEL, POOL_W + 3 * NA_W), D_MODEL ** -0.5),
        "ab_w_out": nrm(ks[10], (N_EVEN, POOL_W + NA_W, D_MODEL), (POOL_W + NA_W) ** -0.5),
        "pool_w": nrm(ks[11], (N_EVEN, N_POOL_GROUPS, POOL_GW, POOL_GW), POOL_GW ** -0.5),
        "pool_scale": 1.0 + nrm(ks[12], (N_EVEN, POOL_W), 0.02),
        "na_rpb": nrm(ks[13], (N_EVEN, NA_HEADS, 2 * NB_ROWS - 1, 2 * NB_COLS - 1), 0.02),
        "rg_w_in": nrm(ks[14], (N_ODD, D_MODEL, 2 * D_RNN), D_MODEL ** -0.5),
        "rg_conv_w": nrm(ks[15], (N_ODD, CONV_W, D_RNN), CONV_W ** -0.5),
        "rg_conv_b": nrm(ks[16], (N_ODD, D_RNN), 0.01),
        "rg_gate_w": nrm(ks[17], (N_ODD, 2, 2, RG_BLOCKS, RG_BW, RG_BW), RG_BW ** -0.5),
        "rg_gate_b": nrm(ks[18], (N_ODD, 2, 2, D_RNN), 0.01),
        "rg_lambda": jnp.log(a_base) - jnp.log1p(-a_base),
        "rg_w_out": nrm(ks[20], (N_ODD, D_RNN, D_MODEL), D_RNN ** -0.5),
        "final_g": 1.0 + nrm(ks[21], (D_MODEL,), 0.02),
    }

def reference(x, c, ctx, c_ctx, ada_w, ada_b, norm_g, ffn_w_gu, ffn_w_down, ab_w_in, ab_w_out,
              pool_w, pool_scale, na_rpb, rg_w_in, rg_conv_w, rg_conv_b, rg_gate_w, rg_gate_b,
              rg_lambda, rg_w_out, final_g):
    B = x.shape[0]
    for i in range(DEPTH):
        last = i == DEPTH - 1
        mx = (jax.nn.silu(c) @ ada_w[i] + ada_b[i]).reshape(B, 1, N_MOD, D_MODEL)
        mc = (jax.nn.silu(c_ctx) @ ada_w[i] + ada_b[i]).reshape(N_MOD, D_MODEL)
        x = x + 0.5 * mx[:, :, 2] * swiglu(modulate(rms_norm(x, norm_g[i, 0]), mx[:, :, 0], mx[:, :, 1]),
                                           ffn_w_gu[i, 0], ffn_w_down[i, 0])
        ctx = ctx + 0.5 * mc[2] * swiglu(modulate(rms_norm(ctx, norm_g[i, 0]), mc[0], mc[1]),
                                         ffn_w_gu[i, 0], ffn_w_down[i, 0])
        hx = modulate(rms_norm(x, norm_g[i, 1]), mx[:, :, 3], mx[:, :, 4])
        hc = modulate(rms_norm(ctx, norm_g[i, 1]), mc[3], mc[4])
        j = i // 2
        if i % 2 == 0:
            yx, yc = pool_nat_mixer(hx, hc, ab_w_in[j], ab_w_out[j], pool_w[j], pool_scale[j],
                                    na_rpb[j], not last)
        else:
            yx, yc = rglru_mixer(hx, hc, rg_w_in[j], rg_conv_w[j], rg_conv_b[j], rg_gate_w[j],
                                 rg_gate_b[j], rg_lambda[j], rg_w_out[j], not last)
        x = x + mx[:, :, 5] * yx
        x = x + 0.5 * mx[:, :, 8] * swiglu(modulate(rms_norm(x, norm_g[i, 2]), mx[:, :, 6], mx[:, :, 7]),
                                           ffn_w_gu[i, 1], ffn_w_down[i, 1])
        if not last:
            ctx = ctx + mc[5] * yc
            ctx = ctx + 0.5 * mc[8] * swiglu(modulate(rms_norm(ctx, norm_g[i, 2]), mc[6], mc[7]),
                                             ffn_w_gu[i, 1], ffn_w_down[i, 1])
    return rms_norm(x, final_g)


_drawn_inputs = setup_inputs


def setup_inputs(seed=0):
    import zlib

    import numpy as np

    out = dict(_drawn_inputs(seed))
    spreads = {}
    factors = {'norm_g': 4.136,
     'pool_scale': 8.0,
     'na_rpb': 64.0,
     'rg_conv_b': 2.923,
     'rg_gate_b': 49.498,
     'final_g': 7.782}
    for name, (base, spread) in spreads.items():
        noise = np.random.default_rng([zlib.crc32(name.encode()), seed]).standard_normal(out[name].shape)
        drawn = base * np.exp(spread * noise) if base else spread * noise
        out[name] = __import__('jax').numpy.asarray(drawn.astype(out[name].dtype))
    for name, factor in factors.items():
        out[name] = (out[name] * factor).astype(out[name].dtype)
    return out
```

```python
from contextlib import ExitStack

import concourse.bass as bass
from concourse import mybir

ALU = mybir.AluOpType
ACT = mybir.ActivationFunctionType
F32 = mybir.dt.float32
F32R = mybir.dt.float32r
AX_X = mybir.AxisListType.X
ds = bass.ds

P = 128
D = 1024
KD = D // P
SEQ = 512
CTX = 256
T = SEQ + CTX
GRID_W = 64
GRID_R = SEQ // GRID_W
DFF = 2816
KF = DFF // P
KC = KF // 2
MODS = 9 * KD
EPS = 1e-6
WINDOWS = (2, 4, 8, 16)
KP = 4
HEADS = 8
DH = 64
NB = 16
SLAB = 32
BLOCKS = GRID_W // NB
RPB_R = 2 * GRID_R - 1
RPB_C = 2 * NB - 1
KR = 10
CONV = 4
RG_C = 8.0

R_ADAB = 0
R_NORM = R_ADAB + 2 * MODS
R_FINAL = R_NORM + 6 * KD
R_PSCALE = R_FINAL + KD
R_CONVW = R_PSCALE + KP
R_CONVB = R_CONVW + CONV * KR
R_GATEB = R_CONVB + KR
R_LAM = R_GATEB + 4 * KR
R_C = R_LAM + 2 * KR
R_CC = R_C + KD
ROWS = R_CC + KD
GROUPS = [(R_C, KD), (R_CC, KD), (R_ADAB, 2 * MODS), (R_NORM, 6 * KD), (R_FINAL, KD), (R_PSCALE, KP),
          (R_CONVW, CONV * KR), (R_CONVB, KR), (R_GATEB, 4 * KR), (R_LAM, 2 * KR)]
ROW_DMAS = sum((r + n - 1) // P - r // P + 1 for r, n in GROUPS)

PAD_X = 8
PAD_C = PAD_X + SEQ + 16
PADW = PAD_C + CTX + 8
TG = PAD_C + CTX - PAD_X
GAP_C = PAD_C - PAD_X

NK = SLAB * GRID_R
SLABS = 2 * BLOCKS
SLAB_AT = [min(max(NB * j - NB // 2, 0), GRID_W - SLAB) for j in range(BLOCKS)]
VARIANT = [0, 1, 1, 2]
SHIFT = [16, 8, 0]
TABLE = 7 * RPB_C + SLAB + 16
SBUF_END = 229344


def trunk(nc, x, c, ctx_in, c_ctx, ada_w, ada_b, norm_g, w_gu, w_down, ab_in, ab_out, pool_w,
          pool_scale, rpb, rg_in, conv_w, conv_b, gate_w, gate_b, lam, rg_out, final_g,
          rpb_pad, rpb_open, v_cols, out):
    stages, first, ktiles = [], {}, []

    def stage(name, panels, kt):
        first[name] = len(ktiles)
        stages.append(name)
        ktiles.extend([kt] * panels)

    def ffn_stages(f):
        for h in range(2):
            stage(f"gu{f}{h}", 2 * KC, KD)
            stage(f"dn{f}{h}", KD, KC)

    ffn_stages(0)
    stage("abin", 16, KD)
    stage("about", KD, KD)
    ffn_stages(1)
    ffn_stages(2)
    first["rg"] = len(ktiles)
    ktiles.extend([KD, KD] + [KD, 4, KD] * (KR - 1) + [4])
    stage("rgout", KD, KR)
    ffn_stages(3)
    NPANELS = len(ktiles)

    ADA0 = 8
    ada_first = {}
    ada = ADA0
    for f in (0, 1):
        for h in range(2):
            ada_first[f"gu{f}{h}"] = ada
            ada_first[f"dn{f}{h}"] = ada + KC
            ada += KC + KD // 2
    ada_first["dn20"] = ada
    ada += KD // 2
    assert ada == MODS

    UPD = {}
    n = 0
    for name in ["in", "dn00", "dn01", "about", "dn10", "dn11", "dn20", "dn21", "rgout", "dn30", "dn31"]:
        UPD[name] = n
        n += KD
    NORMS = ["in", "dn01", "about", "dn11", "dn21", "rgout", "dn31"]

    with ExitStack() as stack:
        top = [16512]

        def at(name, shape, dt, where):
            return nc.alloc_sbuf_tensor_at(name, shape, dt, offset=where)

        def size(shape):
            n = 4
            for s in shape[1:]:
                n *= s
            return (n + 31) // 32 * 32

        def sb(name, shape, dt=F32):
            where = top[0]
            top[0] += size(shape)
            return at(name, shape, dt, where)

        def psum(name, shape):
            return stack.enter_context(nc.psum_tensor(name, shape, F32))

        def sem(name):
            return stack.enter_context(nc.semaphore(name))

        resid = sb("resid", [P, KD, T])
        h_at = top[0]
        hh = sb("h_hi", [P, KD, T], F32R)
        hl = sb("h_lo", [P, KD, T], F32R)
        g_at = top[0]
        gh = sb("g_hi", [P, KC, T], F32R)
        gl = sb("g_lo", [P, KC, T], F32R)
        g_end = top[0]
        raw = sb("raw", [P, 2, KC * P])
        wh = sb("w_hi", [P, 2, KC * P], F32R)
        wl = sb("w_lo", [P, 2, KC * P], F32R)
        ada_at = top[0]
        ada_raw = sb("ada_raw", [P, KD, 2 * P])
        mods = sb("mods", [P, 2 * MODS, 2])
        cols = sb("cols", [P, ROWS])
        mod_a = sb("mod_a", [P, 6, KD, 2])
        mod_g = sb("mod_g", [P, 6, KD, 2])
        cvec = sb("cvec", [P, KD, 2])
        ident = sb("ident", [P, P])
        ones = sb("ones", [P, P])
        rg_scale = sb("rg_scale", [P, 2 * KR])
        rg_tanh = sb("rg_tanh", [P, 2 * KR])
        half_gb = sb("half_gate_bias", [P, 4 * KR])
        lam_s = sb("lam_series", [P, 4, 2 * KR])
        ms = sb("mean_sq", [P, 8])
        sd = sb("std", [P, 8])
        rstd = sb("rstd", [P, 8])
        scr_at = top[0]
        sbuf = sb("work_s", [P, 2, T])
        gbuf = sb("work_g", [P, 2, T])
        acc = sb("sum_sq", [P, T])

        def alias(start, end):
            where = [start]

            def take(name, shape, dt=F32):
                a = where[0]
                where[0] += size(shape)
                assert where[0] <= end, (name, where[0], end)
                return at(name, shape, dt, a)

            return take

        pro = alias(h_at, g_at)
        xin = pro("x_rows", [P, T // P, D])
        rowbuf = pro("vector_rows", [P, 3, P])
        ada0 = alias(g_at, g_end)("ada_first", [P, KD, 2 * ADA0 * P])

        att = alias(g_at, g_end)
        vtok = att("v_tokens", [P, T // P, KP * P])
        vslab = att("v_slabs", [P, SLABS, KP * P])
        qT = att("q_t", [P, KP, T])
        kT = att("k_t", [P, KP, T])
        pT = att("p_t", [P, KP, PADW])
        att_f = at("mixed", [P, 2, T], F32, g_at)
        window = at("window", [P, 2, PADW], F32, scr_at)
        prob = at("prob", [P, 2, 512], F32, scr_at)
        prob_t = at("prob_t", [P, 2, 512], F32, scr_at + size([P, 2, 512]))
        att2 = alias(scr_at + size([P, 4, T]), SBUF_END)
        bias = att2("bias", [P, 2, 3, NK])
        table = att2("rpb_table", [P, 2, TABLE])
        mask = att2("mask", [P, 3, NK])
        rowmax = att2("neg_max", [P, 2])
        rowsum = att2("row_sum", [P, 2])
        rowinv = att2("row_inv", [P, 2])
        inv_n = att2("inv_n", [P, NB])
        first_key = att2("first_key", [P, 4])
        poolw = at("pool_weights", [P, KP, P], F32, ada_at)
        key_col = at("key_col", [P, NK], F32, scr_at)
        key_ge = at("key_ge", [P, NK], F32, scr_at + 4 * NK)
        int_n = at("int_n", [P, NK], mybir.dt.int32, scr_at + 8 * NK)
        int_p = at("int_p", [P, 4], mybir.dt.int32, scr_at + 12 * NK)

        rg = alias(g_at, g_end)
        yh = rg("y_hi", [P, KR, SEQ], F32R)
        yl = rg("y_lo", [P, KR, SEQ], F32R)
        gate_r = [rg(f"gate_r{d}", [P, TG]) for d in range(2)]
        gate_i = [rg(f"gate_i{d}", [P, TG]) for d in range(2)]
        decay = [rg(f"decay{d}", [P, TG]) for d in range(2)]
        root = [rg(f"root{d}", [P, TG]) for d in range(2)]
        rg2 = alias(scr_at, SBUF_END)
        upad = rg2("u_padded", [P, PADW])
        conv = [rg2(f"conv{i}", [P, TG]) for i in range(2)]
        ch = [rg2(f"conv_hi{i}", [P, TG], F32R) for i in range(2)]
        cl = [rg2(f"conv_lo{i}", [P, TG], F32R) for i in range(2)]
        yf = rg2("y_f32", [P, SEQ])
        rg3 = alias(ada_at, ada_at + size([P, KD, 2 * P]))
        gel_q = rg3("gelu_square", [P, SEQ])
        gel_z = rg3("gelu_inner", [P, SEQ])
        gel = rg3("gelu", [P, 2, SEQ])

        pA = psum("pair_a", [P, 2 * 512])
        pB = psum("pair_b", [P, 2 * 512])
        pC = psum("pair_c", [P, 2 * 512])
        pR = psum("pair_r", [P, 2 * 512])
        pair = [pA, pB]

        raw_landed = [sem("raw_landed0"), sem("raw_landed1")]
        hi_done = sem("hi_done")
        split_ready = sem("split_ready")
        panel_used = sem("panel_used")
        silu_done = sem("silu_done")
        gate_up_done = sem("gate_up_done")
        g_hi_done = sem("g_hi_done")
        g_split_done = sem("g_split_done")
        resid_done = sem("resid_done")
        square_done = sem("square_done")
        sum_done = sem("sum_done")
        ss_done = sem("ss_done")
        ms_done = sem("ms_done")
        sd_done = sem("sd_done")
        rstd_done = sem("rstd_done")
        diag_done = sem("diag_done")
        rbc_done = sem("rbc_done")
        scaled_done = sem("scaled_done")
        mod_done = sem("mod_done")
        h_hi_done = sem("h_hi_done")
        h_ready = sem("h_ready")
        ada_landed = sem("ada_landed")
        ada_used = sem("ada_used")
        mods_done = sem("mods_done")
        coef_done = sem("coef_done")
        rows_landed = sem("rows_landed")
        x_landed = sem("x_landed")
        ada0_landed = sem("ada0_landed")
        const_done = sem("const_done")
        cols_t = sem("cols_t")
        cols_done = sem("cols_done")
        cvec_done = sem("cvec_done")
        xt_done = sem("xt_done")
        out_t = sem("out_t")
        out_copied = sem("out_copied")
        out_stored = sem("out_stored")


        proj_done = sem("proj_done")
        v_stored = sem("v_stored")
        v_loaded = sem("v_loaded")
        rpb_padded = sem("rpb_padded")
        rpb_opened = sem("rpb_opened")
        table_landed = [sem("table_landed0"), sem("table_landed1")]
        iota_done = sem("iota_done")
        mask_done = sem("mask_done")
        bias_done = sem("bias_done")
        poolw_landed = sem("poolw_landed")
        pooled_done = sem("pooled_done")
        poolmm_done = sem("poolmm_done")
        mixed_done = sem("mixed_done")
        mixed_hi = sem("mixed_hi")
        mixed_split = sem("mixed_split")
        scores_done = sem("scores_done")
        max_done = sem("max_done")
        prob_done = sem("prob_done")
        prob_scaled = sem("prob_scaled")
        turned_done = sem("turned_done")
        prob_t_done = sem("prob_t_done")
        pv_done = sem("pv_done")
        dve_step = sem("dve_step")
        act_step = sem("act_step")
        u_done = sem("u_done")
        conv_done = sem("conv_done")
        conv_hi = sem("conv_hi")
        conv_split = sem("conv_split")
        gelu_q = sem("gelu_q")
        gelu_z = sem("gelu_z")
        gelu_t = sem("gelu_t")
        gelu_done = sem("gelu_done")
        gates_done = sem("gates_done")
        decay_done = sem("decay_done")
        root_done = sem("root_done")
        scan_done = sem("scan_done")
        y_done = sem("y_done")
        y_hi_done = sem("y_hi_done")
        y_split = sem("y_split")
        final_scaled = sem("final_scaled")
        lam_exp = sem("lam_exp")
        rg_ready = sem("rg_ready")

        block = stack.enter_context(nc.Block())

        def chained(engine, done):
            count = [0]

            def link(instruction):
                instruction.then_inc(done, 1)
                count[0] += 1
                engine.wait_ge(done, count[0])

            return link

        def ada_seen(q):
            return q - (ADA0 - 2)

        NORM_AT = {name: i for i, name in enumerate(NORMS)}
        SITE = {"dn00": 0, "dn01": 0, "about": 1, "dn10": 2, "dn11": 2, "dn20": 3, "dn21": 3,
                "rgout": 4, "dn30": 5, "dn31": 5}
        X_ONLY = ("rgout", "dn30", "dn31")
        GU_BEFORE = {(f, h): (2 * f + h) * KC for f in range(4) for h in range(2)}


        def shift_tile(site):
            return 3 * KD * site

        def u_panel(n):
            return P_RG if n == 0 else P_RG + 3 * n - 1

        def g_panel(n):
            return P_RG + 1 if n == 0 else P_RG + 3 * n + 1

        def gate_panel(n):
            return min(P_RG + 3 * (n + 1), P_RG + 3 * KR - 1)

        P_AB, P_ABOUT, P_RG, P_RGOUT = first["abin"], first["about"], first["rg"], first["rgout"]
        STEPS = [(h, j) for h in range(HEADS) for j in range(BLOCKS + 2)]

        @block.sync
        def _(sp):
            landed = [0]

            def span(start, n):
                return ds(start if isinstance(start, int) else sp.snap(start), n)


            def rows(src, r, count):
                a = 0
                while a < count:
                    t, q = divmod(r + a, P)
                    k = min(count - a, P - q)
                    sp.dma_start(rowbuf[q:q + k, t, :], src[a:a + k, :]).then_inc(rows_landed, 16)
                    landed[0] += 1
                    a += k

            rows(c.rearrange("b (k p) -> (b k) p", p=P), R_C, KD)
            rows(c_ctx.rearrange("(k p) -> k p", p=P), R_CC, KD)
            rows(ada_b.rearrange("l (k p) -> (l k) p", p=P), R_ADAB, 2 * MODS)
            rows(norm_g.rearrange("l s (k p) -> (l s k) p", p=P), R_NORM, 6 * KD)
            rows(final_g.rearrange("(k p) -> k p", p=P), R_FINAL, KD)
            rows(pool_scale.rearrange("o (k p) -> (o k) p", p=P), R_PSCALE, KP)
            rows(conv_w.rearrange("o w (k p) -> (o w k) p", p=P), R_CONVW, CONV * KR)
            rows(conv_b.rearrange("o (k p) -> (o k) p", p=P), R_CONVB, KR)
            rows(gate_b.rearrange("o d g (k p) -> (o d g k) p", p=P), R_GATEB, 4 * KR)
            rows(lam.rearrange("o d (k p) -> (o d k) p", p=P), R_LAM, 2 * KR)
            assert landed[0] == ROW_DMAS, landed[0]
            xt = x[0].rearrange("(t p) n -> p t n", p=P)
            sp.dma_start(xin[:, 0:SEQ // P, :], xt).then_inc(x_landed, 16)
            sp.dma_start(xin[:, SEQ // P:T // P, :], ctx_in[0].rearrange("(t p) n -> p t n", p=P)).then_inc(x_landed, 16)
            w0 = ada_w[0].rearrange("(k p) n -> p k n", p=P)
            for i in range(4):
                w = 2 * ADA0 * P // 4
                sp.dma_start(ada0[:, :, i * w:(i + 1) * w], w0[:, :, i * w:(i + 1) * w]).then_inc(ada0_landed, 16)

            def load(p, par, kt, src):
                if not isinstance(p, int) or p >= 2:
                    sp.wait_ge(split_ready, p - 1)
                sp.dma_start(raw[:, par, 0:kt * P].rearrange("p (k n) -> p k n", n=P), src).then_inc(raw_landed[par], 16)

            def load_ada(q, col, layer):
                w = ada_w[layer].rearrange("(k p) n -> p k n", p=P)[:, :, span(col * (2 * P), 2 * P)]
                sp.wait_ge(ada_used, q - (ADA0 - 1))
                sp.dma_start(ada_raw[:, :, :], w).then_inc(ada_landed, 16)

            def with_ada(q0, start, count, body):
                cuts = [start, count]
                if q0 is not None and q0 + start < MODS // 2 < q0 + count:
                    cuts = [start, MODS // 2 - q0, count]
                for a, b in zip(cuts, cuts[1:]):
                    with sp.Fori(a, b) as i:
                        if q0 is not None:
                            layer = (q0 + a) // (MODS // 2)
                            load_ada(i + q0, i + (q0 - layer * (MODS // 2)), layer)
                        body(i)

            def ffn(f):
                layer, which = divmod(f, 2)
                gu = w_gu[layer, which].rearrange("(k p) n -> p k n", p=P)
                dn = w_down[layer, which].rearrange("(k p) n -> p k n", p=P)
                for h in range(2):
                    p0 = first[f"gu{f}{h}"]

                    def gate_up(i):
                        load(i * 2 + p0, 0, KD, gu[:, :, span(i * P + h * KC * P, P)])
                        load(i * 2 + (p0 + 1), 1, KD, gu[:, :, span(i * P + (DFF + h * KC * P), P)])

                    if p0 == 0:
                        load(0, 0, KD, gu[:, :, 0:P])
                        load(1, 1, KD, gu[:, :, DFF:DFF + P])
                        load_ada(ADA0, ADA0, 0)
                        pad_rpb()
                    with_ada(ada_first.get(f"gu{f}{h}"), int(p0 == 0), KC, gate_up)
                    p0 = first[f"dn{f}{h}"]

                    def down(i):
                        for r in range(2):
                            load(i * 2 + (p0 + r), r, KC, dn[:, h * KC:(h + 1) * KC, span(i * (2 * P) + r * P, P)])

                    with_ada(ada_first.get(f"dn{f}{h}"), 0, KD // 2, down)

            def pad_rpb():
                flat = rpb.rearrange("o h r c -> o (h r c)")
                n = HEADS * RPB_R * RPB_C
                sp.dma_start(rpb_pad[:, 16:16 + n], flat).then_inc(rpb_padded, 16)
                sp.dma_start(rpb_pad[:, 0:16], flat[:, 0:16]).then_inc(rpb_padded, 16)
                sp.dma_start(rpb_pad[:, 16 + n:32 + n], flat[:, 0:16]).then_inc(rpb_padded, 16)

            def open_rpb():
                sp.wait_ge(rpb_padded, 48)
                for h in range(HEADS):
                    src = bass.AP(tensor=rpb_pad.tensor, offset=h * RPB_R * RPB_C, ap=[[1, NB], [RPB_C, GRID_R], [1, TABLE]])
                    sp.dma_start(rpb_open[h].rearrange("(c r) n -> c r n", r=GRID_R), src).then_inc(rpb_opened, 16)

            ffn(0)

            win = ab_in[0].rearrange("(k p) n -> p k n", p=P)
            order = [0, 3, 2, 1]
            for n in range(4):
                if n == 1:
                    sp.wait_ge(ada_used, ada_seen(ada_first["gu10"] - 1))
                    sp.dma_start(poolw[:, :, :], pool_w[0].rearrange("g k j -> k g j")).then_inc(poolw_landed, 16)
                    open_rpb()
                with sp.Fori(0, 2) as i:
                    for r in range(2):
                        load(i * 2 + (P_AB + 4 * n + r), r, KD, win[:, :, span(i * (2 * P) + (order[n] * KP + r) * P, P)])
            sp.wait_ge(proj_done, 2 + 8)
            vc = v_cols.rearrange("(c r) n -> r c n", r=GRID_R)
            for r in range(GRID_R):
                sp.dma_start(vc[r], vtok[GRID_W * (r % 2):GRID_W * (r % 2 + 1), r // 2, :]).then_inc(v_stored, 16)
            sp.wait_ge(v_stored, 16 * GRID_R)
            for j in range(BLOCKS):
                src = v_cols[SLAB_AT[j] * GRID_R:SLAB_AT[j] * GRID_R + NK, :].rearrange("(t p) n -> p t n", p=P)
                sp.dma_start(vslab[:, 2 * j:2 * j + 2, :], src).then_inc(v_loaded, 16)
            wout = ab_out[0].rearrange("(k p) n -> p k n", p=P)
            sp.wait_ge(rpb_opened, 16 * HEADS)
            for h in range(HEADS):
                if h >= 2:
                    sp.wait_ge(bias_done, h - 1)
                sp.dma_start(table[:, h % 2, :], rpb_open[h]).then_inc(table_landed[h % 2], 16)
                if h == 1:
                    for r in range(2):
                        load(P_ABOUT + r, r, KD, wout[:, :, r * P:(r + 1) * P])
            with sp.Fori(1, KD // 2) as i:
                for r in range(2):
                    load(i * 2 + (P_ABOUT + r), r, KD, wout[:, :, span(i * (2 * P) + r * P, P)])

            ffn(1)
            ffn(2)

            rin = rg_in[0].rearrange("(k p) n -> p k n", p=P)
            gw = gate_w[0].rearrange("d g n k j -> n k (d g) j")
            DR = KR * P

            def load_u(p, par, n):
                load(p, par, KD, rin[:, :, span(n * P + DR, P)])

            def load_g(p, par, n):
                src = rin[:, :, 0:P] if isinstance(n, int) and n == 0 else rin[:, :, P:DR][:, :, ds((n - 1) * P, P)]
                load(p, par, KD, src)

            def load_gates(p, par, n):
                src = gw[ds(n, 1)].rearrange("o k b j -> (o k) b j")
                load(p, par, 4, src)

            load_u(P_RG, 0, 0)
            load_g(P_RG + 1, 1, 0)
            with sp.Fori(0, KR // 2 - 1) as i:
                for b in range(2):
                    p = i * 6 + (P_RG + 2 + 3 * b)
                    load_u(p, b, i * 2 + (b + 1))
                    load_gates(p + 1, 1 - b, i * 2 + b)
                    load_g(p + 2, b, i * 2 + (b + 1))
            p = P_RG + 3 * KR - 4
            load_u(p, 0, KR - 1)
            load_gates(p + 1, 1, KR - 2)
            load_g(p + 2, 0, KR - 1)
            load_gates(p + 3, 1, KR - 1)
            wro = rg_out[0].rearrange("(k p) n -> p k n", p=P)
            with sp.Fori(0, KD // 2) as i:
                for r in range(2):
                    load(i * 2 + (P_RGOUT + r), r, KR, wro[:, :, span(i * (2 * P) + r * P, P)])

            ffn(3)
            for half in range(2):
                sp.wait_ge(out_copied, KD // 2 * (half + 1))
                n0 = half * (D // 2)
                sp.dma_start(out[0].rearrange("(t p) n -> p t n", p=P)[:, :, n0:n0 + D // 2],
                             xin[:, 0:SEQ // P, n0:n0 + D // 2]).then_inc(out_stored, 16)
            sp.wait_ge(out_stored, 32)

        @block.gpsimd
        def _(pool):
            nc.gpsimd.memset(ident[:, :], 0.0).then_inc(const_done, 1)
            nc.gpsimd.memset(ones[:, :], 1.0).then_inc(const_done, 1)
            pool.wait_ge(const_done, 1)
            nc.gpsimd.affine_select(out=ident[:, :], in_=ident[:, :], compare_op=ALU.not_equal, fill=1.0, base=0,
                                    pattern=[[-1, P]], channel_multiplier=1).then_inc(const_done, 1)

            def low(p, par, kt):
                pool.wait_ge(hi_done, p + 1)
                nc.gpsimd.tensor_tensor(wl[:, par, 0:kt * P], raw[:, par, 0:kt * P],
                                        wh[:, par, 0:kt * P].bitcast(F32), ALU.subtract).then_inc(split_ready, 1)

            def pairs(p0, start, count, kt):
                with pool.Fori(start, count) as i:
                    for r in range(2):
                        low(i * 2 + (p0 + r), r, kt)

            def norm(name):
                i = NORM_AT[name]
                W = SEQ if name in X_ONLY else T
                for k in range(KD):
                    pool.wait_ge(h_hi_done, i * KD + k + 1)
                    nc.gpsimd.tensor_tensor(hl[:, k, 0:W], gbuf[:, k % 2, 0:W], hh[:, k, 0:W].bitcast(F32),
                                            ALU.subtract).then_inc(h_ready, 1)

            def ffn(f, after):
                low(first[f"gu{f}0"], 0, KD)
                low(first[f"gu{f}0"] + 1, 1, KD)
                norm(after)
                pairs(first[f"gu{f}0"], 1, KC, KD)
                pairs(first[f"dn{f}0"], 0, KD // 2, KC)
                pairs(first[f"gu{f}1"], 0, KC, KD)
                pairs(first[f"dn{f}1"], 0, KD // 2, KC)

            ffn(0, "in")
            low(P_AB, 0, KD)
            low(P_AB + 1, 1, KD)
            norm("dn01")
            pool.wait_ge(h_ready, (NORM_AT["dn01"] + 1) * KD)
            nc.gpsimd.iota(int_n[:, :], [[1, SLAB], [0, GRID_R]], base=0, channel_multiplier=0).then_inc(iota_done, 1)
            nc.gpsimd.iota(int_p[:, 0:1], [[0, 1]], base=0, channel_multiplier=1).then_inc(iota_done, 1)
            pairs(P_AB, 1, 8, KD)
            for h in range(HEADS):
                if h == 2:
                    low(P_ABOUT, 0, KD)
                    low(P_ABOUT + 1, 1, KD)
                pool.wait_ge(table_landed[h % 2], 16 * (h // 2 + 1))
                pool.wait_ge(mask_done, 1)
                if h >= 2:
                    pool.wait_ge(scores_done, (BLOCKS + 2) * (h - 2) + BLOCKS)
                for v in range(3):
                    t = bass.AP(tensor=table[:, :, :].tensor, offset=table[:, h % 2, SHIFT[v]:SHIFT[v] + 1].offset,
                                ap=[list(table[:, 0, 0:1].ap[0]), [1, SLAB], [RPB_C, GRID_R]])
                    last = nc.gpsimd.tensor_tensor(bias[:, h % 2, v, :].rearrange("p (c r) -> p c r", r=GRID_R), t,
                                                   mask[:, v, :].rearrange("p (c r) -> p c r", r=GRID_R), ALU.add)
                last.then_inc(bias_done, 1)
            pairs(P_ABOUT, 1, KD // 2, KD)
            ffn(1, "about")
            ffn(2, "dn11")
            low(P_RG, 0, KD)
            low(P_RG + 1, 1, KD)
            norm("dn21")

            def conv_low(n):
                pool.wait_ge(conv_hi, n + 1)
                nc.gpsimd.tensor_tensor(cl[n % 2][:, :], conv[n % 2][:, :], ch[n % 2][:, :].bitcast(F32),
                                        ALU.subtract).then_inc(conv_split, 1)

            def y_low(n):
                pool.wait_ge(y_hi_done, n + 1)
                nc.gpsimd.tensor_tensor(yl[:, n, :], yf[:, :], yh[:, n, :].bitcast(F32),
                                        ALU.subtract).then_inc(y_split, 1)

            conv_low(0)
            for n in range(1, KR):
                p = P_RG + 3 * n - 1
                low(p, (n + 1) % 2, KD)
                low(p + 1, n % 2, 4)
                low(p + 2, (n + 1) % 2, KD)
                if n >= 2:
                    y_low(n - 2)
                conv_low(n)
            low(P_RG + 3 * KR - 1, 1, 4)
            y_low(KR - 2)
            low(P_RGOUT, 0, KR)
            low(P_RGOUT + 1, 1, KR)
            y_low(KR - 1)
            pairs(P_RGOUT, 1, KD // 2, KR)
            ffn(3, "rgout")

        @block.scalar
        def _(act):
            chain = chained(act, act_step)

            def high(p, par=None):
                kt = KD
                if isinstance(p, int):
                    if p >= NPANELS:
                        return
                    par, kt = p % 2, ktiles[p]
                    land = 16 * (p // 2 + 1)
                    if p >= 2:
                        act.wait_ge(panel_used, p - 1)
                    act.wait_ge(raw_landed[par], land)
                nc.scalar.activation(wh[:, par, 0:kt * P], raw[:, par, 0:kt * P], ACT.Copy).then_inc(hi_done, 1)

            def silu(F, p):
                act.wait_ge(panel_used, p + 1)
                act.wait_ge(gate_up_done, F + 1)
                if f_width[0] == T:
                    nc.scalar.activation(sbuf[:, 0, :], pA[:, 0:T], ACT.Silu).then_inc(silu_done, 1)
                else:
                    nc.scalar.activation(sbuf[:, 0, 0:SEQ], pA[:, 0:SEQ], ACT.Silu).then_inc(silu_done, 1)

            f_width = [T]

            def gate_up(f, h):
                f_width[0] = SEQ if f == 3 else T
                p0, F0 = first[f"gu{f}{h}"], GU_BEFORE[f, h]
                with act.Fori(0, KC - 1) as i:
                    silu(i + F0, i * 2 + p0)
                    for r in range(2):
                        act.wait_ge(panel_used, i * 2 + (p0 + r + 1))
                        act.wait_ge(raw_landed[r], i * 16 + 16 * ((p0 + r) // 2 + 2))
                        high(None, r)
                silu(KC - 1 + F0, 2 * (KC - 1) + p0)
                high(p0 + 2 * KC)
                high(p0 + 2 * KC + 1)

            def square(name, k):
                i = NORM_AT[name]
                W = SEQ if name in X_ONLY else T
                act.wait_ge(resid_done, UPD[name] + k + 1)
                if k >= 3:
                    act.wait_ge(sum_done, i * (KD - 1) + k - 2)
                dst = acc if k == 0 else sbuf[:, k % 2, :]
                nc.scalar.activation(dst[:, 0:W], resid[:, k, 0:W], ACT.Square).then_inc(square_done, 1)

            def norm(name):
                i = NORM_AT[name]
                W = SEQ if name in X_ONLY else T
                n = W // P
                act.wait_ge(ms_done, i + 1)
                nc.scalar.activation(sd[:, 0:n], ms[:, 0:n], ACT.Sqrt).then_inc(sd_done, 1)
                if name == "dn31":
                    for k in range(KD):
                        act.wait_ge(scaled_done, i * KD + k + 1)
                        if k >= 2:
                            act.wait_ge(out_t, k - 1)
                        nc.scalar.activation(gbuf[:, k % 2, 0:SEQ], sbuf[:, k % 2, 0:SEQ], ACT.Copy,
                                             scale=cols[:, R_FINAL + k:R_FINAL + k + 1]).then_inc(final_scaled, 1)
                    return
                site = i
                act.wait_ge(coef_done, 3 * site + 2)
                for k in range(KD):
                    act.wait_ge(scaled_done, i * KD + k + 1)
                    if i * KD + k >= 2:
                        act.wait_ge(h_ready, i * KD + k - 1)
                    t = shift_tile(site) + k
                    last = nc.scalar.activation(gbuf[:, k % 2, 0:SEQ], sbuf[:, k % 2, 0:SEQ], ACT.Identity,
                                                bias=mods[:, t, 0:1], scale=mod_a[:, site, k, 0:1])
                    if W == T:
                        last = nc.scalar.activation(gbuf[:, k % 2, SEQ:T], sbuf[:, k % 2, SEQ:T], ACT.Identity,
                                                    bias=mods[:, t, 1:2], scale=mod_a[:, site, k, 1:2])
                    last.then_inc(mod_done, 1)
                    act.wait_ge(mod_done, i * KD + k + 1)
                    nc.scalar.activation(hh[:, k, 0:W], gbuf[:, k % 2, 0:W], ACT.Copy).then_inc(h_hi_done, 1)

            def copy_turned(s):
                j, b = STEPS[s][1], s % 2
                W = NK + CTX if j < BLOCKS else CTX
                act.wait_ge(turned_done, s + 1)
                if s >= 2:
                    act.wait_ge(pv_done, s - 1)
                nc.scalar.activation(prob_t[:, b, 0:W], pB[:, b * 512:b * 512 + W], ACT.Copy).then_inc(prob_t_done, 1)

            def outputs(name, p0):
                if name in NORM_AT:
                    chain(nc.scalar.activation(sd[:, 7:8], ones[:, 0:1], ACT.Sqrt))
                for k in range(KD):
                    high(p0 + k + 2)
                    if name in NORM_AT:
                        square(name, k)

            def ffn(f):
                for h in range(2):
                    gate_up(f, h)
                    outputs(f"dn{f}{h}", first[f"dn{f}{h}"])
                norm(f"dn{f}1")

            act.wait_ge(cols_done, 1)
            for v, r in ((0, R_C), (1, R_CC)):
                last = nc.scalar.activation(cvec[:, :, v], cols[:, r:r + KD], ACT.Silu)
            last.then_inc(silu_done, 1)
            act.wait_ge(const_done, 3)
            chain(nc.scalar.activation(sd[:, 7:8], ones[:, 0:1], ACT.Sqrt))
            high(0)
            high(1)
            for k in range(KD):
                square("in", k)
            norm("in")
            act.wait_ge(lam_exp, 1)
            nc.scalar.activation(lam_s[:, 1, :], lam_s[:, 0, :], ACT.Exp, scale=-1.0).then_inc(lam_exp, 1)
            ffn(0)

            for j in range(16):
                high(P_AB + j + 2)
            for g in range(KP):
                act.wait_ge(poolmm_done, g + 1)
                act.wait_ge(v_stored, 16 * GRID_R)
                if g >= 2:
                    act.wait_ge(mixed_split, g - 1)
                ps = pC if g % 2 == 0 else pR
                nc.scalar.activation(att_f[:, g % 2, :], ps[:, 0:T], ACT.Copy,
                                     scale=cols[:, R_PSCALE + g:R_PSCALE + g + 1]).then_inc(mixed_done, 1)
                act.wait_ge(mixed_done, g + 1)
                nc.scalar.activation(hh[:, g, :], att_f[:, g % 2, :], ACT.Copy).then_inc(mixed_hi, 1)
            for s, (h, j) in enumerate(STEPS):
                W = NK + CTX if j < BLOCKS else CTX
                b = s % 2
                act.wait_ge(max_done, s + 1)
                if s >= 2:
                    act.wait_ge(turned_done, s - 1)
                nc.scalar.activation(prob[:, b, 0:W], pA[:, b * 512:b * 512 + W], ACT.Exp, bias=rowmax[:, b:b + 1],
                                     accum_out=rowsum[:, b:b + 1]).then_inc(prob_done, 1)
                if s >= 1:
                    copy_turned(s - 1)
            copy_turned(len(STEPS) - 1)
            outputs("about", P_ABOUT)
            norm("about")
            ffn(1)
            ffn(2)

            def u_rows(n):
                act.wait_ge(panel_used, u_panel(n) + 1)
                if n == 0:
                    act.wait_ge(rg_ready, 1)
                else:
                    act.wait_ge(conv_done, n)
                nc.scalar.activation(upad[:, PAD_X:PAD_X + SEQ], pA[:, 0:SEQ], ACT.Copy)
                nc.scalar.activation(upad[:, PAD_C:PAD_C + CTX], pA[:, 512:512 + CTX], ACT.Copy).then_inc(u_done, 1)

            def gelu_rows(n):
                act.wait_ge(panel_used, g_panel(n) + 1)
                if n >= 1:
                    act.wait_ge(gelu_done, n)
                nc.scalar.activation(gel_q[:, :], pB[:, 0:SEQ], ACT.Square, scale=0.044715 ** 0.5).then_inc(gelu_q, 1)

            def gelu_tanh(n):
                act.wait_ge(gelu_z, n + 1)
                nc.scalar.activation(gel_q[:, :], gel_z[:, :], ACT.Tanh, scale=(2 / 3.141592653589793) ** 0.5)\
                    .then_inc(gelu_t, 1)

            def gates(n):
                act.wait_ge(panel_used, gate_panel(n) + 1)
                if n == 0:
                    act.wait_ge(rg_ready, 2)
                else:
                    act.wait_ge(decay_done, 2 * n)
                for g, dst in enumerate((gate_r, gate_i)):
                    for d in range(2):
                        xp, x0 = ((pB, 512), (pC, 0), (pR, 0), (pR, 512))[2 * d + g]
                        cc, c0 = (pC, 512) if d == 0 else (pA, 512)
                        half = half_gb[:, (2 * d + g) * KR + n:(2 * d + g) * KR + n + 1]
                        if g == 1 and n >= 1:
                            act.wait_ge(scan_done, 2 * (n - 1) + d + 1)
                        nc.scalar.activation(dst[d][:, 0:SEQ], xp[:, x0:x0 + SEQ], ACT.Tanh, bias=half, scale=0.5)
                        nc.scalar.activation(dst[d][:, GAP_C:TG], cc[:, c0 + g * CTX:c0 + (g + 1) * CTX], ACT.Tanh,
                                             bias=half, scale=0.5).then_inc(gates_done, 1)
                act.wait_ge(gates_done, 4 * n + 2)
                if n >= 1:
                    act.wait_ge(y_done, n)
                for d in range(2):
                    m = d * KR + n
                    nc.scalar.activation(decay[d][:, :], gate_r[d][:, :], ACT.Exp, bias=rg_scale[:, m:m + 1],
                                         scale=rg_scale[:, m:m + 1])
                    nc.scalar.activation(root[d][:, :], gate_r[d][:, :], ACT.Tanh, bias=rg_tanh[:, m:m + 1],
                                         scale=rg_tanh[:, m:m + 1]).then_inc(decay_done, 1)
                for d in range(2):
                    act.wait_ge(decay_done, 2 * n + d + 1)
                    nc.scalar.activation(root[d][:, :], root[d][:, :], ACT.Sqrt, scale=0.25).then_inc(root_done, 1)

            high(P_RG + 2)
            u_rows(0)
            high(P_RG + 3)
            gelu_rows(0)
            gelu_tanh(0)
            for n in range(1, KR):
                high(P_RG + 3 * n + 1)
                u_rows(n)
                high(P_RG + 3 * n + 2)
                gates(n - 1)
                high(P_RG + 3 * n + 3)
                gelu_rows(n)
                gelu_tanh(n)
            high(P_RG + 3 * KR + 1)
            gates(KR - 1)
            outputs("rgout", P_RGOUT)
            norm("rgout")
            ffn(3)

        @block.vector
        def _(dve):
            chain = chained(dve, dve_step)

            def coef_a(site):
                layer, j = divmod(site, 3)
                t = shift_tile(site) + KD
                r = R_NORM + (layer * 3 + j) * KD
                for v in range(2):
                    nc.vector.scalar_tensor_tensor(out=mod_a[:, site, :, v], in0=mods[:, t:t + KD, v], scalar=1.0,
                                                   in1=cols[:, r:r + KD], op0=ALU.add, op1=ALU.mult)\
                        .then_inc(coef_done, 1)

            def coef_g(site):
                t = shift_tile(site) + 2 * KD
                nc.vector.tensor_scalar(mod_g[:, site, :, :], mods[:, t:t + KD, :], 1.0 if site % 3 == 1 else 0.5, None,
                                        ALU.mult).then_inc(coef_done, 1)

            def take_ada(q):
                dve.wait_ge(ada_used, q - (ADA0 - 2))
                src = pC[:, 0:4].rearrange("p (t v) -> p v t", v=2)
                for v in range(2):
                    last = nc.vector.tensor_tensor(mods[:, ds(q * 2, 2), v], src[:, v, :], cols[:, ds(q * 2, 2)], ALU.add)
                last.then_inc(mods_done, 1)

            def gate_up(f, h):
                W = SEQ if f == 3 else T
                p0, F0 = first[f"gu{f}{h}"], GU_BEFORE[f, h]
                q0 = ada_first.get(f"gu{f}{h}")
                with dve.Fori(0, KC) as i:
                    if q0 is not None:
                        take_ada(i + q0)
                    dve.wait_ge(silu_done, i + (F0 + 2))
                    dve.wait_ge(panel_used, i * 2 + (p0 + 2))
                    dve.wait_ge(g_split_done, i + (F0 + 1))
                    nc.vector.tensor_tensor(gbuf[:, 0, 0:W], sbuf[:, 0, 0:W], pB[:, 0:W], ALU.mult)\
                        .then_inc(gate_up_done, 1)
                    dve.wait_ge(gate_up_done, i + (F0 + 2))
                    nc.vector.tensor_copy(gh[:, ds(i, 1), 0:W].rearrange("p o n -> p (o n)"), gbuf[:, 0, 0:W])\
                        .then_inc(g_hi_done, 1)
                    dve.wait_ge(g_hi_done, i + (F0 + 1))
                    nc.vector.tensor_tensor(gl[:, ds(i, 1), 0:W].rearrange("p o n -> p (o n)"), gbuf[:, 0, 0:W],
                                            gh[:, ds(i, 1), 0:W].rearrange("p o n -> p (o n)").bitcast(F32),
                                            ALU.subtract).then_inc(g_split_done, 1)

            def add_square(name, k):
                i = NORM_AT[name]
                W = SEQ if name in X_ONLY else T
                dve.wait_ge(square_done, i * KD + k + 1)
                if k >= 2:
                    dve.wait_ge(sum_done, i * (KD - 1) + k - 1)
                nc.vector.tensor_tensor(acc[:, 0:W], acc[:, 0:W], sbuf[:, k % 2, 0:W], ALU.add).then_inc(sum_done, 1)

            def outputs(name, p0):
                site = SITE[name]
                if name[:2] != "dn" or name[3] == "0":
                    dve.wait_ge(mods_done, ada_seen((shift_tile(site) + 3 * KD) // 2 - 1))
                    coef_g(site)
                    dve.wait_ge(coef_done, 3 * site + 3)
                q0 = ada_first.get(name)
                for k in range(KD):
                    if q0 is not None and k % 2 == 0:
                        take_ada_static(q0 + k // 2)
                    dve.wait_ge(panel_used, p0 + k + 1)
                    ps = pair[k % 2]
                    last = nc.vector.scalar_tensor_tensor(out=resid[:, k, 0:SEQ], in0=ps[:, 0:SEQ],
                                                          scalar=mod_g[:, site, k, 0:1], in1=resid[:, k, 0:SEQ],
                                                          op0=ALU.mult, op1=ALU.add)
                    if name not in X_ONLY:
                        last = nc.vector.scalar_tensor_tensor(out=resid[:, k, SEQ:T], in0=ps[:, 512:512 + CTX],
                                                              scalar=mod_g[:, site, k, 1:2], in1=resid[:, k, SEQ:T],
                                                              op0=ALU.mult, op1=ALU.add)
                    last.then_inc(resid_done, 1)
                    if name in NORM_AT and k >= 2:
                        add_square(name, k - 1)
                if name in NORM_AT:
                    add_square(name, KD - 1)

            def take_ada_static(q):
                dve.wait_ge(ada_used, ada_seen(q))
                src = pC[:, 0:4].rearrange("p (t v) -> p v t", v=2)
                for v in range(2):
                    last = nc.vector.tensor_tensor(mods[:, 2 * q:2 * q + 2, v], src[:, v, :], cols[:, 2 * q:2 * q + 2],
                                                   ALU.add)
                last.then_inc(mods_done, 1)

            def norm(name):
                i = NORM_AT[name]
                W = SEQ if name in X_ONLY or name == "dn31" else T
                n = W // P
                if name != "dn31":
                    dve.wait_ge(mods_done, ada_seen((shift_tile(i) + 2 * KD) // 2 - 1))
                    coef_a(i)
                dve.wait_ge(ss_done, i + 1)
                nc.vector.tensor_scalar(ms[:, 0:n], pC[:, 512:512 + n], 1.0 / D, EPS, ALU.mult, ALU.add)\
                    .then_inc(ms_done, 1)
                dve.wait_ge(sd_done, i + 1)
                nc.vector.reciprocal(rstd[:, 0:n], sd[:, 0:n]).then_inc(rstd_done, 1)
                dve.wait_ge(rstd_done, i + 1)
                for t in range(n):
                    last = nc.vector.tensor_scalar(acc[:, t * P:(t + 1) * P], ident[:, :], rstd[:, t:t + 1], None,
                                                   ALU.mult)
                last.then_inc(diag_done, 1)
                dve.wait_ge(rbc_done, i + 1)
                for k in range(KD):
                    if k >= 2:
                        dve.wait_ge(mod_done if name != "dn31" else final_scaled, (i * KD if name != "dn31" else 0) + k - 1)
                    nc.vector.tensor_tensor(sbuf[:, k % 2, 0:W], resid[:, k, 0:W], pR[:, 0:W], ALU.mult)\
                        .then_inc(scaled_done, 1)
                    if name == "dn31" and k >= 1:
                        copy_out(k - 1)
                if name == "dn31":
                    copy_out(KD - 1)

            def copy_out(k):
                dve.wait_ge(out_t, k + 1)
                nc.vector.tensor_copy(xin[:, 0:SEQ // P, k * P:(k + 1) * P],
                                      pair[k % 2][:, 0:SEQ].rearrange("p (t n) -> p t n", n=P)).then_inc(out_copied, 1)

            def ffn(f):
                for h in range(2):
                    gate_up(f, h)
                    outputs(f"dn{f}{h}", first[f"dn{f}{h}"])
                norm(f"dn{f}1")

            dve.wait_ge(cols_t, 1)
            nc.vector.tensor_copy(cols[:, :], pR[:, 0:ROWS]).then_inc(cols_done, 1)
            dve.wait_ge(cols_done, 1)
            nc.vector.tensor_scalar(half_gb[:, :], cols[:, R_GATEB:R_GATEB + 4 * KR], 0.5, None, ALU.mult)\
                .then_inc(gate_up_done, 1)
            nc.vector.tensor_scalar(lam_s[:, 2, :], cols[:, R_LAM:R_LAM + 2 * KR], -1.0, None, ALU.mult)\
                .then_inc(g_split_done, 1)
            dve.wait_ge(g_split_done, 1)
            nc.vector.tensor_tensor(lam_s[:, 0, :], cols[:, R_LAM:R_LAM + 2 * KR], lam_s[:, 2, :], ALU.max)\
                .then_inc(lam_exp, 1)
            for k in range(KD):
                dve.wait_ge(xt_done, k + 1)
                nc.vector.tensor_copy(resid[:, k, :], pair[k % 2][:, 0:T]).then_inc(resid_done, 1)
                if k >= 2:
                    add_square("in", k - 1)
            add_square("in", KD - 1)
            dve.wait_ge(ada_used, 1)
            src = pC[:, 0:4 * ADA0].rearrange("p (t v) -> p v t", v=2)
            for v in range(2):
                last = nc.vector.tensor_tensor(mods[:, 0:2 * ADA0, v], src[:, v, :], cols[:, 0:2 * ADA0], ALU.add)
            last.then_inc(mods_done, 1)
            norm("in")
            dve.wait_ge(lam_exp, 2)
            e, z, w = lam_s[:, 1, :], lam_s[:, 3, :], lam_s[:, 0, :]
            chain(nc.vector.tensor_scalar(z, e, 2.0, None, ALU.add))
            chain(nc.vector.reciprocal(w, z))
            chain(nc.vector.tensor_tensor(z, e, w, ALU.mult))
            chain(nc.vector.tensor_tensor(w, z, z, ALU.mult))
            chain(nc.vector.tensor_scalar(e, w, 1.0 / 19, None, ALU.mult))
            for m in range(17, 1, -2):
                chain(nc.vector.scalar_tensor_tensor(out=e, in0=e, scalar=1.0 / m, in1=w, op0=ALU.add, op1=ALU.mult))
            chain(nc.vector.scalar_tensor_tensor(out=e, in0=e, scalar=1.0, in1=z, op0=ALU.add, op1=ALU.mult))
            chain(nc.vector.tensor_scalar(w, lam_s[:, 2, :], 0.0, None, ALU.max))
            chain(nc.vector.scalar_tensor_tensor(out=w, in0=e, scalar=2.0, in1=w, op0=ALU.mult, op1=ALU.add))
            chain(nc.vector.tensor_scalar(rg_scale[:, :], w, -RG_C / 2, None, ALU.mult))
            chain(nc.vector.tensor_scalar(rg_tanh[:, :], w, RG_C / 4, None, ALU.mult))
            ffn(0)

            nc.vector.memset(pT[:, :, 0:PAD_X], 0.0)
            nc.vector.memset(pT[:, :, PADW - 8:PADW], 0.0).then_inc(proj_done, 1)
            nc.vector.memset(pT[:, :, PAD_X + SEQ:PAD_C], 0.0).then_inc(proj_done, 1)

            def column_major(ps):
                return ps[:, 0:SEQ].rearrange("p (r c) -> p c r", c=GRID_W)

            def project(j):
                n, m = divmod(j, KP)
                ps = pair[j % 2]
                dve.wait_ge(panel_used, P_AB + j + 1)
                if n == 0:
                    nc.vector.tensor_copy(pT[:, m, PAD_X:PAD_X + SEQ], ps[:, 0:SEQ])
                    last = nc.vector.tensor_copy(pT[:, m, PAD_C:PAD_C + CTX], ps[:, 512:512 + CTX])
                elif n == 1:
                    last = nc.vector.tensor_copy(vtok[:, :, m * P:(m + 1) * P], ps[:, 0:T].rearrange("p (t n) -> p t n", n=P))
                else:
                    dst, scale = (kT, 1.0) if n == 2 else (qT, DH ** -0.5)
                    to = dst[:, m, 0:SEQ] if n == 2 else dst[:, m, 0:SEQ][:, ::-1]
                    nc.vector.tensor_scalar(to.rearrange("p (c r) -> p c r", r=GRID_R), column_major(ps),
                                            scale, None, ALU.mult)
                    last = nc.vector.tensor_scalar(dst[:, m, SEQ:T], ps[:, 512:512 + CTX], scale, None, ALU.mult)
                last.then_inc(proj_done, 1)

            def masks():
                dve.wait_ge(iota_done, 2)
                chain(nc.vector.tensor_scalar(int_p[:, 1:2], int_p[:, 0:1], 3, None, ALU.arith_shift_right))
                chain(nc.vector.tensor_copy(first_key[:, 3:4], int_p[:, 1:2]))
                chain(nc.vector.tensor_scalar(first_key[:, 1:2], first_key[:, 3:4], -1.0, NB - 1.0, ALU.mult, ALU.add))
                chain(nc.vector.tensor_copy(key_col[:, :], int_n[:, :]))
                chain(nc.vector.tensor_scalar(first_key[:, 0:1], first_key[:, 1:2], -8.0, 0.0, ALU.add, ALU.max))
                chain(nc.vector.tensor_scalar(first_key[:, 2:3], first_key[:, 1:2], 8.0, 16.0, ALU.add, ALU.min))
                for v in range(3):
                    chain(nc.vector.tensor_scalar(key_ge[:, :], key_col[:, :], first_key[:, v:v + 1], None, ALU.is_ge))
                    chain(nc.vector.tensor_scalar(first_key[:, 3:4], first_key[:, v:v + 1], float(NB), None, ALU.add))
                    chain(nc.vector.scalar_tensor_tensor(out=mask[:, v, :], in0=key_col[:, :], scalar=first_key[:, 3:4],
                                                              in1=key_ge[:, :], op0=ALU.is_lt, op1=ALU.mult))
                    chain(nc.vector.tensor_scalar(mask[:, v, :], mask[:, v, :], -1.0, 1e30, ALU.add, ALU.mult))
                chain(nc.vector.tensor_scalar(inv_n[:, :], key_col[:, 0:NB * GRID_R:GRID_R], 1.0, None, ALU.add))
                nc.vector.reciprocal(inv_n[:, :], inv_n[:, :]).then_inc(mask_done, 1)
                dve.wait_ge(mask_done, 1)

            def pool_group(g):
                w = WINDOWS[g]
                u = pT[:, g, :]
                if g >= 1:
                    dve.wait_ge(pooled_done, g)
                chain(nc.vector.tensor_tensor(window[:, 0, 1:PADW], u[:, 0:PADW - 1], u[:, 1:PADW], ALU.add))
                reach, cur, lo, hi = 1, 0, 1, PADW
                while 2 * reach < w:
                    a, b = lo + reach, hi - reach
                    chain(nc.vector.tensor_tensor(window[:, 1 - cur, a:b], window[:, cur, a - reach:b - reach],
                                                       window[:, cur, a + reach:b + reach], ALU.add))
                    lo, hi, reach, cur = a, b, 2 * reach, 1 - cur
                half = w // 2
                for at_, length in ((PAD_X, SEQ), (PAD_C, CTX)):
                    left = window[:, cur, at_:at_ + half]
                    chain(nc.vector.scalar_tensor_tensor(out=left, in0=left, scalar=float(w), in1=inv_n[:, half - 1:w - 1],
                                                              op0=ALU.mult, op1=ALU.mult))
                    if half > 1:
                        right = window[:, cur, at_ + length - half + 1:at_ + length]
                        chain(nc.vector.scalar_tensor_tensor(out=right, in0=right, scalar=float(w),
                                                                  in1=inv_n[:, half:w - 1][:, ::-1],
                                                                  op0=ALU.mult, op1=ALU.mult))
                nc.vector.scalar_tensor_tensor(out=u[:, PAD_X:PAD_C + CTX], in0=window[:, cur, PAD_X:PAD_C + CTX],
                                               scalar=1.0 / w, in1=u[:, PAD_X:PAD_C + CTX], op0=ALU.mult,
                                               op1=ALU.subtract).then_inc(pooled_done, 1)

            for j in range(16):
                project(j)
                if j == 4:
                    masks()
                if 5 <= j < 5 + KP:
                    pool_group(j - 5)
            for g in range(KP):
                dve.wait_ge(mixed_hi, g + 1)
                nc.vector.tensor_tensor(hl[:, g, :], att_f[:, g % 2, :], hh[:, g, :].bitcast(F32), ALU.subtract)\
                    .then_inc(mixed_split, 1)

            def normalise(s):
                h, j = STEPS[s]
                W = NK + CTX if j < BLOCKS else CTX
                b = s % 2
                dve.wait_ge(prob_done, s + 1)
                chain(nc.vector.reciprocal(rowinv[:, b:b + 1], rowsum[:, b:b + 1]))
                nc.vector.tensor_scalar(prob[:, b, 0:W], prob[:, b, 0:W], rowinv[:, b:b + 1], None, ALU.mult)\
                    .then_inc(prob_scaled, 1)

            def take_heads(t):
                dve.wait_ge(pv_done, (2 * t + 2) * (BLOCKS + 2))
                f = att_f[:, t % 2, :]
                o, oc = pC[:, (t % 2) * 512:(t % 2) * 512 + SEQ], pR[:, (t % 2) * 512:(t % 2) * 512 + CTX]
                nc.vector.tensor_copy(f[:, 0:SEQ].rearrange("p (r c) -> p r c", c=GRID_W),
                                      o[:, ::-1].rearrange("p (c r) -> p r c", r=GRID_R))
                chain(nc.vector.tensor_copy(f[:, SEQ:T], oc))
                chain(nc.vector.tensor_copy(hh[:, KP + t, :], f))
                nc.vector.tensor_tensor(hl[:, KP + t, :], f, hh[:, KP + t, :].bitcast(F32), ALU.subtract)\
                    .then_inc(mixed_split, 1)

            for s, (h, j) in enumerate(STEPS):
                W = NK + CTX if j < BLOCKS else CTX
                b = s % 2
                dve.wait_ge(scores_done, s + 1)
                nc.vector.reduce_max(rowmax[:, b:b + 1], pA[:, b * 512:b * 512 + W], AX_X, negate=True)\
                    .then_inc(max_done, 1)
                if s >= 1:
                    normalise(s - 1)
                if j == 3 and h % 2 == 0 and h >= 2:
                    take_heads(h // 2 - 1)
            normalise(len(STEPS) - 1)
            take_heads(3)
            outputs("about", P_ABOUT)
            norm("about")
            ffn(1)
            ffn(2)

            dve.wait_ge(panel_used, P_RG + 1)
            nc.vector.memset(upad[:, :], 0.0).then_inc(rg_ready, 1)
            for d in range(2):
                nc.vector.memset(gate_r[d][:, :], 0.0)
                last = nc.vector.memset(gate_i[d][:, :], 0.0)
            last.then_inc(rg_ready, 1)

            def convolve(n):
                dve.wait_ge(u_done, n + 1)
                if n >= 1:
                    dve.wait_ge(conv_split, n)
                cw = [cols[:, R_CONVW + k * KR + n:R_CONVW + k * KR + n + 1] for k in range(CONV)]
                cb = cols[:, R_CONVB + n:R_CONVB + n + 1]
                a = PAD_X - CONV // 2
                chain(nc.vector.tensor_scalar(conv[n % 2][:, :], upad[:, a:a + TG], cw[0], cb, ALU.mult, ALU.add))
                for k in range(1, CONV):
                    ins = nc.vector.scalar_tensor_tensor(out=conv[n % 2][:, :], in0=upad[:, a + k:a + k + TG], scalar=cw[k],
                                                         in1=conv[n % 2][:, :], op0=ALU.mult, op1=ALU.add)
                    if k < CONV - 1:
                        chain(ins)
                ins.then_inc(conv_done, 1)
                dve.wait_ge(conv_done, n + 1)
                if n >= 2:
                    dve.wait_ge(panel_used, gate_panel(n - 2) + 1)
                nc.vector.tensor_copy(ch[n % 2][:, :], conv[n % 2][:, :]).then_inc(conv_hi, 1)

            def gelu(n):
                dve.wait_ge(gelu_q, n + 1)
                nc.vector.scalar_tensor_tensor(out=gel_z[:, :], in0=gel_q[:, :], scalar=1.0, in1=pB[:, 0:SEQ],
                                               op0=ALU.add, op1=ALU.mult).then_inc(gelu_z, 1)
                dve.wait_ge(gelu_t, n + 1)
                nc.vector.scalar_tensor_tensor(out=gel[:, n % 2, :], in0=gel_q[:, :], scalar=1.0, in1=pB[:, 0:SEQ],
                                               op0=ALU.add, op1=ALU.mult).then_inc(gelu_done, 1)

            def recur(n):
                for d in range(2):
                    dve.wait_ge(gates_done, 4 * n + 3 + d)
                    chain(nc.vector.scalar_tensor_tensor(out=gate_i[d][:, :], in0=gate_i[d][:, :], scalar=1.0,
                                                              in1=conv[n % 2][:, :], op0=ALU.add, op1=ALU.mult))
                for d in range(2):
                    a, b = decay[d], gate_i[d]
                    dve.wait_ge(root_done, 2 * n + d + 1)
                    chain(nc.vector.scalar_tensor_tensor(out=root[d][:, :], in0=a[:, :], scalar=1.0,
                                                              in1=root[d][:, :], op0=ALU.add, op1=ALU.mult))
                    chain(nc.vector.tensor_tensor(b[:, :], b[:, :], root[d][:, :], ALU.mult))
                    step, end = (1, TG - 1) if d == 0 else (-1, GAP_C)
                    ac, bc = a[:, GAP_C:TG][:, ::step], b[:, GAP_C:TG][:, ::step]
                    chain(nc.vector.tensor_tensor_scan(ac, ac, bc, 0.0, ALU.mult, ALU.add))
                    ax, bx = a[:, 0:SEQ][:, ::step], b[:, 0:SEQ][:, ::step]
                    nc.vector.tensor_tensor_scan(ax, ax, bx, a[:, end:end + 1], ALU.mult, ALU.add).then_inc(scan_done, 1)
                dve.wait_ge(scan_done, 2 * n + 2)
                chain(nc.vector.tensor_tensor(decay[0][:, 0:SEQ], decay[0][:, 0:SEQ], decay[1][:, 0:SEQ], ALU.add))
                if n >= 1:
                    dve.wait_ge(y_split, n)
                dve.wait_ge(gelu_done, n + 1)
                nc.vector.scalar_tensor_tensor(out=yf[:, :], in0=gel[:, n % 2, :], scalar=0.5, in1=decay[0][:, 0:SEQ],
                                               op0=ALU.mult, op1=ALU.mult).then_inc(y_done, 1)
                dve.wait_ge(y_done, n + 1)
                nc.vector.tensor_copy(yh[:, n, :], yf[:, :]).then_inc(y_hi_done, 1)

            convolve(0)
            gelu(0)
            for n in range(1, KR):
                convolve(n)
                recur(n - 1)
                gelu(n)
            recur(KR - 1)
            outputs("rgout", P_RGOUT)
            norm("rgout")
            ffn(3)

        @block.tensor
        def _(pe):
            def passes(dst, par, kk, hi, lo, start, stop):
                w1, w2 = wh[:, par, kk * P:(kk + 1) * P], wl[:, par, kk * P:(kk + 1) * P]
                nc.tensor.matmul(dst, w1, hi, start=start, stop=False)
                nc.tensor.matmul(dst, w1, lo, start=False, stop=False)
                return nc.tensor.matmul(dst, w2, hi, start=False, stop=stop)

            def panel(ps, par, kt, hi, lo, W, each=None):
                for k in range(kt):
                    if each:
                        each(k)
                    last = passes(ps[:, 0:SEQ], par, k, hi[:, k, 0:SEQ], lo[:, k, 0:SEQ], k == 0, k == kt - 1)
                    if W == T:
                        last = passes(ps[:, 512:512 + CTX], par, k, hi[:, k, SEQ:T], lo[:, k, SEQ:T], k == 0, k == kt - 1)
                last.then_inc(panel_used, 1)

            def use_ada(q):
                pe.wait_ge(ada_landed, (q - (ADA0 - 1)) * 16)
                pe.wait_ge(mods_done, q - (ADA0 - 1))
                for t in range(2):
                    for k in range(KD):
                        last = nc.tensor.matmul(pC[:, 2 * t:2 * t + 2], ada_raw[:, k, t * P:(t + 1) * P], cvec[:, k, :],
                                                start=(k == 0), stop=(k == KD - 1))
                last.then_inc(ada_used, 1)

            def after_norm(name):
                i = NORM_AT[name]
                return lambda k: pe.wait_ge(h_ready, i * KD + k + 1)

            def gate_up(f, h, each):
                W = SEQ if f == 3 else T
                p0, F0 = first[f"gu{f}{h}"], GU_BEFORE[f, h]
                q0 = ada_first.get(f"gu{f}{h}")
                with pe.Fori(0, KC) as i:
                    if q0 is not None:
                        use_ada(i + q0)
                    pe.wait_ge(split_ready, i * 2 + (p0 + 1))
                    pe.wait_ge(silu_done, i + (F0 + 1))
                    if h == 1:
                        pe.wait_ge(resid_done, UPD[f"dn{f}0"] + KD - 1)
                    panel(pA, 0, KD, hh, hl, W, each)
                    pe.wait_ge(split_ready, i * 2 + (p0 + 2))
                    pe.wait_ge(gate_up_done, i + (F0 + 1))
                    if h == 1:
                        pe.wait_ge(resid_done, UPD[f"dn{f}0"] + KD)
                    panel(pB, 1, KD, hh, hl, W)

            def outputs(name, p0, kt, hi, lo):
                W = SEQ if name in X_ONLY else T
                q0 = ada_first.get(name)
                with pe.Fori(0, KD // 2) as i:
                    if q0 is not None:
                        use_ada(i + q0)
                    for r in range(2):
                        pe.wait_ge(split_ready, i * 2 + (p0 + r + 1))
                        pe.wait_ge(resid_done, i * 2 + (UPD[name] + r - 1))
                        panel(pair[r], r, kt, hi, lo, W)

            def norm(name):
                i = NORM_AT[name]
                W = SEQ if name in X_ONLY or name == "dn31" else T
                pe.wait_ge(sum_done, (i + 1) * (KD - 1))
                for t in range(W // P):
                    last = nc.tensor.matmul(pC[:, 512 + t:513 + t], acc[:, t * P:(t + 1) * P], ones[:, 0:1],
                                            start=True, stop=True)
                last.then_inc(ss_done, 1)
                pe.wait_ge(diag_done, i + 1)
                last = nc.tensor.matmul(pR[:, 0:SEQ], ones[:, :], acc[:, 0:SEQ], start=True, stop=True)
                if W == T:
                    last = nc.tensor.matmul(pR[:, 512:512 + CTX], ones[:, :], acc[:, SEQ:T], start=True, stop=True)
                last.then_inc(rbc_done, 1)

            def ffn(f, after):
                for h in range(2):
                    gate_up(f, h, after_norm(after) if h == 0 else None)
                    pe.wait_ge(g_split_done, GU_BEFORE[f, h] + KC + 1)
                    outputs(f"dn{f}{h}", first[f"dn{f}{h}"], KC, gh, gl)
                norm(f"dn{f}1")

            pe.wait_ge(const_done, 3)
            pe.wait_ge(rows_landed, 16 * ROW_DMAS)
            for t in range(3):
                n = min(P, ROWS - t * P)
                last = nc.tensor.transpose(pR[:, t * P:t * P + n], rowbuf[0:n, t, :], ident[0:n, 0:n])
            last.then_inc(cols_t, 1)
            pe.wait_ge(x_landed, 32)
            for k in range(KD):
                if k >= 2:
                    pe.wait_ge(resid_done, k - 1)
                for t in range(T // P):
                    last = nc.tensor.transpose(pair[k % 2][:, t * P:(t + 1) * P], xin[:, t, k * P:(k + 1) * P],
                                               ident[:, :])
                last.then_inc(xt_done, 1)
            pe.wait_ge(silu_done, 1)
            pe.wait_ge(ada0_landed, 64)
            for t in range(2 * ADA0):
                for k in range(KD):
                    last = nc.tensor.matmul(pC[:, 2 * t:2 * t + 2], ada0[:, k, t * P:(t + 1) * P], cvec[:, k, :],
                                            start=(k == 0), stop=(k == KD - 1))
            last.then_inc(ada_used, 1)
            pe.wait_ge(cols_done, 1)
            norm("in")
            ffn(0, "in")

            def tokens_on_partitions(ps, par):
                for t in range(T // P):
                    for k in range(KD):
                        w1, w2 = wh[:, par, k * P:(k + 1) * P], wl[:, par, k * P:(k + 1) * P]
                        h1, h2 = hh[:, k, t * P:(t + 1) * P], hl[:, k, t * P:(t + 1) * P]
                        dst = ps[:, t * P:(t + 1) * P]
                        nc.tensor.matmul(dst, h1, w1, start=(k == 0), stop=False)
                        nc.tensor.matmul(dst, h1, w2, start=False, stop=False)
                        last = nc.tensor.matmul(dst, h2, w1, start=False, stop=(k == KD - 1))
                last.then_inc(panel_used, 1)

            for n in range(4):
                with pe.Fori(0, 2) as i:
                    for r in range(2):
                        pe.wait_ge(split_ready, i * 2 + (P_AB + 4 * n + r + 1))
                        pe.wait_ge(proj_done, i * 2 + (4 * n + r + 1))
                        if n == 1:
                            tokens_on_partitions(pair[r], r)
                        else:
                            panel(pair[r], r, KD, hh, hl, T, after_norm("dn01") if n == 0 and r == 0 else None)
            pe.wait_ge(poolw_landed, 16)
            for g in range(KP):
                pe.wait_ge(pooled_done, g + 1)
                if g >= 2:
                    pe.wait_ge(mixed_done, g - 1)
                ps = pC if g % 2 == 0 else pR
                nc.tensor.matmul(ps[:, 0:SEQ], poolw[:, g, :], pT[:, g, PAD_X:PAD_X + SEQ], start=True, stop=True)
                nc.tensor.matmul(ps[:, 512:512 + CTX], poolw[:, g, :], pT[:, g, PAD_C:PAD_C + CTX], start=True,
                                 stop=True).then_inc(poolmm_done, 1)

            def scores(s):
                h, j = STEPS[s]
                t, a = divmod(h, 2)
                rows = slice(a * DH, (a + 1) * DH)
                b = s % 2
                if s >= 2:
                    pe.wait_ge(prob_done, s - 1)
                else:
                    pe.wait_ge(proj_done, 2 + 16)
                bank = pA[:, b * 512:(b + 1) * 512]
                if j < BLOCKS:
                    q = qT[rows, t, (BLOCKS - 1 - j) * P:(BLOCKS - j) * P]
                    if j == 0:
                        pe.wait_ge(bias_done, h + 1)
                    k0 = SLAB_AT[j] * GRID_R
                    nc.tensor.matmul(bank[:, 0:NK], q, kT[rows, t, k0:k0 + NK], start=True, stop=False)
                    nc.tensor.matmul(bank[:, 0:NK], ident[:, :], bias[:, h % 2, VARIANT[j], :], start=False, stop=True)
                    last = nc.tensor.matmul(bank[:, NK:NK + CTX], q, kT[rows, t, SEQ:T], start=True, stop=True)
                else:
                    q = qT[rows, t, j * P:(j + 1) * P]
                    last = nc.tensor.matmul(bank[:, 0:CTX], q, kT[rows, t, SEQ:T], start=True, stop=True)
                last.then_inc(scores_done, 1)

            def turn(s):
                h, j = STEPS[s]
                b = s % 2
                pe.wait_ge(prob_scaled, s + 1)
                if s >= 2:
                    pe.wait_ge(prob_t_done, s - 1)
                for t in range(4 if j < BLOCKS else 2):
                    last = nc.tensor.transpose(pB[:, b * 512 + t * P:b * 512 + (t + 1) * P], prob[:, b, t * P:(t + 1) * P],
                                               ident[:, :])
                last.then_inc(turned_done, 1)

            def values(s):
                h, j = STEPS[s]
                t, a = divmod(h, 2)
                rows = slice(a * DH, (a + 1) * DH)
                b = s % 2
                pe.wait_ge(prob_t_done, s + 1)
                if s == 0:
                    pe.wait_ge(v_loaded, 16 * BLOCKS)
                    pe.wait_ge(mixed_done, KP)
                if j == 0 and a == 0 and t >= 2:
                    pe.wait_ge(mixed_split, KP + t - 1)
                if j < BLOCKS:
                    c0 = (t % 2) * 512 + (BLOCKS - 1 - j) * P
                    dst = pC[rows, c0:c0 + P]
                    tiles = [vslab[:, 2 * j, h * DH:(h + 1) * DH], vslab[:, 2 * j + 1, h * DH:(h + 1) * DH]]
                else:
                    dst = pR[rows, (t % 2) * 512 + (j - BLOCKS) * P:(t % 2) * 512 + (j - BLOCKS + 1) * P]
                    tiles = []
                tiles += [vtok[:, SEQ // P + i, h * DH:(h + 1) * DH] for i in range(2)]
                for i, v in enumerate(tiles):
                    last = nc.tensor.matmul(dst, v, prob_t[:, b, i * P:(i + 1) * P], start=(i == 0),
                                            stop=(i == len(tiles) - 1))
                last.then_inc(pv_done, 1)

            n = len(STEPS)
            scores(0)
            for s in range(n):
                if s + 1 < n:
                    scores(s + 1)
                if s >= 1:
                    values(s - 1)
                turn(s)
            values(n - 1)
            pe.wait_ge(mixed_split, 2 * KP)
            outputs("about", P_ABOUT, KD, hh, hl)
            norm("about")
            ffn(1, "about")
            ffn(2, "dn11")

            def u_rows(p, par, n, each=None):
                pe.wait_ge(split_ready, p + 1)
                if n is not None:
                    pe.wait_ge(u_done, n)
                panel(pA, par, KD, hh, hl, T, each)

            def g_rows(p, par, n):
                pe.wait_ge(split_ready, p + 1)
                if n is not None:
                    pe.wait_ge(gelu_done, n)
                panel(pB, par, KD, hh, hl, SEQ)

            def gates(p, par, b, n):
                pe.wait_ge(split_ready, p + 1)
                pe.wait_ge(conv_split, n + 1)
                for d in range(2):
                    xr, xi = (pB[:, 512:1024], pC[:, 0:512]) if d == 0 else (pR[:, 0:512], pR[:, 512:1024])
                    cc = pC[:, 512:1024] if d == 0 else pA[:, 512:1024]
                    for g in range(2):
                        passes(xr if g == 0 else xi, par, 2 * d + g, ch[b][:, 0:SEQ], cl[b][:, 0:SEQ], True, True)
                    for g in range(2):
                        last = passes(cc[:, g * CTX:(g + 1) * CTX], par, 2 * d + g, ch[b][:, GAP_C:TG],
                                      cl[b][:, GAP_C:TG], True, True)
                last.then_inc(panel_used, 1)

            u_rows(P_RG, 0, None, after_norm("dn21"))
            g_rows(P_RG + 1, 1, None)
            u_rows(P_RG + 2, 0, 1)
            pe.wait_ge(u_done, 2)
            gates(P_RG + 3, 1, 0, 0)
            g_rows(P_RG + 4, 0, 1)
            with pe.Fori(0, KR // 2 - 1) as i:
                for b in range(2):
                    p = i * 6 + (P_RG + 5 + 3 * b)
                    pe.wait_ge(gates_done, i * 8 + 4 * (b + 1))
                    u_rows(p, 1 - b, i * 2 + (2 + b))
                    pe.wait_ge(u_done, i * 2 + (3 + b))
                    gates(p + 1, b, 1 - b, i * 2 + (1 + b))
                    g_rows(p + 2, 1 - b, i * 2 + (2 + b))
            pe.wait_ge(gates_done, 4 * (KR - 1))
            gates(P_RG + 3 * KR - 1, 1, (KR - 1) % 2, KR - 1)
            pe.wait_ge(y_split, KR)
            outputs("rgout", P_RGOUT, KR, yh, yl)
            norm("rgout")
            ffn(3, "rgout")
            for k in range(KD):
                pe.wait_ge(final_scaled, k + 1)
                if k >= 2:
                    pe.wait_ge(out_copied, k - 1)
                for t in range(SEQ // P):
                    last = nc.tensor.transpose(pair[k % 2][:, t * P:(t + 1) * P], gbuf[:, k % 2, t * P:(t + 1) * P],
                                               ident[:, :])
                last.then_inc(out_t, 1)


_INS = ['x', 'c', 'ctx', 'c_ctx', 'ada_w', 'ada_b', 'norm_g', 'ffn_w_gu', 'ffn_w_down', 'ab_w_in', 'ab_w_out', 'pool_w',
        'pool_scale', 'na_rpb', 'rg_w_in', 'rg_conv_w', 'rg_conv_b', 'rg_gate_w', 'rg_gate_b', 'rg_lambda', 'rg_w_out',
        'final_g']


def kernel(**inputs):
    import numpy as _np
    import concourse.bacc as _bacc
    from concourse.bass_utils import run_bass_kernel_spmd as _run

    nc = _bacc.Bacc("TRN2", target_bir_lowering=False, num_devices=1)
    arrays, args = {}, []
    for name in _INS:
        a = _np.ascontiguousarray(inputs[name])
        arrays[f"in_{name}_dram"] = a
        args.append(nc.dram_tensor(f"in_{name}_dram", a.shape, F32, kind="ExternalInput").ap())
    args.append(nc.dram_tensor("rpb_padded_dram", (1, 32 + HEADS * RPB_R * RPB_C), F32, kind="Internal").ap())
    args.append(nc.dram_tensor("rpb_opened_dram", (HEADS, P, TABLE), F32, kind="Internal").ap())
    args.append(nc.dram_tensor("v_columns_dram", (SEQ, KP * P), F32, kind="Internal").ap())
    args.append(nc.dram_tensor("out_0_dram", (1, SEQ, D), F32, kind="ExternalOutput").ap())
    trunk(nc, *args)
    r = _run(nc, [arrays], core_ids=[0])
    return r.results[0]["out_0_dram"]
```

```python
from contextlib import ExitStack

import concourse.bass as bass
from concourse import mybir

ALU = mybir.AluOpType
ACT = mybir.ActivationFunctionType
F32 = mybir.dt.float32
F32R = mybir.dt.float32r
AX_X = mybir.AxisListType.X
ds = bass.ds

P = 128
D = 1024
KD = D // P
SEQ = 512
CTX = 256
T = SEQ + CTX
GRID_W = 64
GRID_R = SEQ // GRID_W
DFF = 2816
KF = DFF // P
KC = KF // 2
MODS = 9 * KD
EPS = 1e-6
WINDOWS = (2, 4, 8, 16)
KP = 4
HEADS = 8
DH = 64
NB = 16
SLAB = 32
BLOCKS = GRID_W // NB
RPB_R = 2 * GRID_R - 1
RPB_C = 2 * NB - 1
KR = 10
CONV = 4
RG_C = 8.0

R_ADAB = 0
R_NORM = R_ADAB + 2 * MODS
R_FINAL = R_NORM + 6 * KD
R_PSCALE = R_FINAL + KD
R_CONVW = R_PSCALE + KP
R_CONVB = R_CONVW + CONV * KR
R_GATEB = R_CONVB + KR
R_LAM = R_GATEB + 4 * KR
R_C = R_LAM + 2 * KR
R_CC = R_C + KD
ROWS = R_CC + KD
GROUPS = [(R_C, KD), (R_CC, KD), (R_ADAB, 2 * MODS), (R_NORM, 6 * KD), (R_FINAL, KD), (R_PSCALE, KP),
          (R_CONVW, CONV * KR), (R_CONVB, KR), (R_GATEB, 4 * KR), (R_LAM, 2 * KR)]
ROW_DMAS = sum((r + n - 1) // P - r // P + 1 for r, n in GROUPS)

PAD_X = 8
PAD_C = PAD_X + SEQ + 16
PADW = PAD_C + CTX + 8
TG = PAD_C + CTX - PAD_X
GAP_C = PAD_C - PAD_X

NK = SLAB * GRID_R
SLABS = 2 * BLOCKS
SLAB_AT = [min(max(NB * j - NB // 2, 0), GRID_W - SLAB) for j in range(BLOCKS)]
VARIANT = [0, 1, 1, 2]
SHIFT = [16, 8, 0]
TABLE = 7 * RPB_C + SLAB + 16
SBUF_END = 229344


def trunk(nc, x, c, ctx_in, c_ctx, ada_w, ada_b, norm_g, w_gu, w_down, ab_in, ab_out, pool_w,
          pool_scale, rpb, rg_in, conv_w, conv_b, gate_w, gate_b, lam, rg_out, final_g,
          rpb_pad, rpb_open, v_cols, out):
    stages, first, ktiles = [], {}, []

    def stage(name, panels, kt):
        first[name] = len(ktiles)
        stages.append(name)
        ktiles.extend([kt] * panels)

    def ffn_stages(f):
        for h in range(2):
            stage(f"gu{f}{h}", 2 * KC, KD)
            stage(f"dn{f}{h}", KD, KC)

    ffn_stages(0)
    stage("abin", 16, KD)
    stage("about", KD, KD)
    ffn_stages(1)
    ffn_stages(2)
    first["rg"] = len(ktiles)
    ktiles.extend([KD, KD] + [KD, 4, KD] * (KR - 1) + [4])
    stage("rgout", KD, KR)
    ffn_stages(3)
    NPANELS = len(ktiles)

    ADA0 = 8
    ADA0_W = ADA0 // 4 * 2 * P
    ada_first = {}
    ada = ADA0
    for f in (0, 1):
        for h in range(2):
            ada_first[f"gu{f}{h}"] = ada
            ada_first[f"dn{f}{h}"] = ada + KC
            ada += KC + KD // 2
    ada_first["dn20"] = ada
    ada += KD // 2
    assert ada == MODS

    UPD = {}
    n = 0
    for name in ["in", "dn00", "dn01", "about", "dn10", "dn11", "dn20", "dn21", "rgout", "dn30", "dn31"]:
        UPD[name] = n
        n += KD
    NORMS = ["in", "dn01", "about", "dn11", "dn21", "rgout", "dn31"]

    with ExitStack() as stack:
        top = [16512]

        def at(name, shape, dt, where):
            return nc.alloc_sbuf_tensor_at(name, shape, dt, offset=where)

        def size(shape):
            n = 4
            for s in shape[1:]:
                n *= s
            return (n + 31) // 32 * 32

        def sb(name, shape, dt=F32):
            where = top[0]
            top[0] += size(shape)
            return at(name, shape, dt, where)

        def psum(name, shape):
            return stack.enter_context(nc.psum_tensor(name, shape, F32))

        def sem(name):
            return stack.enter_context(nc.semaphore(name))

        resid = sb("resid", [P, KD, T])
        h_at = top[0]
        hh = sb("h_hi", [P, KD, T], F32R)
        hl = sb("h_lo", [P, KD, T], F32R)
        g_at = top[0]
        gh = sb("g_hi", [P, KC, T], F32R)
        gl = sb("g_lo", [P, KC, T], F32R)
        g_end = top[0]
        raw = sb("raw", [P, 2, KC * P])
        wh = sb("w_hi", [P, 2, KC * P], F32R)
        wl = sb("w_lo", [P, 2, KC * P], F32R)
        ada_at = top[0]
        ada_raw = sb("ada_raw", [P, KD, 2 * P])
        mods = sb("mods", [P, 2 * MODS, 2])
        cols = sb("cols", [P, ROWS])
        mod_a = sb("mod_a", [P, 6, KD, 2])
        mod_g = sb("mod_g", [P, 6, KD, 2])
        cvec = sb("cvec", [P, KD, 2])
        ident = sb("ident", [P, P])
        ones = sb("ones", [P, P])
        rg_scale = sb("rg_scale", [P, 2 * KR])
        rg_tanh = sb("rg_tanh", [P, 2 * KR])
        half_gb = sb("half_gate_bias", [P, 4 * KR])
        lam_s = sb("lam_series", [P, 4, 2 * KR])
        ms = sb("mean_sq", [P, 8])
        sd = sb("std", [P, 8])
        rstd = sb("rstd", [P, 8])
        scr_at = top[0]
        sbuf = sb("work_s", [P, 2, T])
        gbuf = sb("work_g", [P, 2, T])
        normed = [sbuf[:, 0, :], sbuf[:, 1, :], gbuf[:, 0, :], gbuf[:, 1, :]]
        acc = sb("sum_sq", [P, T])
        ada_sum = sb("ada_sums", [P, 2, 2 * P])

        def alias(start, end):
            where = [start]

            def take(name, shape, dt=F32):
                a = where[0]
                where[0] += size(shape)
                assert where[0] <= end, (name, where[0], end)
                return at(name, shape, dt, a)

            return take

        pro = alias(h_at, g_at)
        xin = pro("x_rows", [P, T // P, D])
        rowbuf = pro("vector_rows", [P, 3, P])
        ada0_sum = pro("ada_first_sums", [P, 2, 2, ADA0_W])
        ada0 = alias(g_at, g_end)("ada_first", [P, KD, 2 * ADA0 * P])

        att = alias(g_at, g_end)
        vtok = att("v_tokens", [P, T // P, KP * P])
        vslab = att("v_slabs", [P, SLABS, KP * P])
        qT = att("q_t", [P, KP, T])
        kT = att("k_t", [P, KP, T])
        pT = att("p_t", [P, KP, PADW])
        att_f = at("mixed", [P, 2, T], F32, g_at)
        window = at("window", [P, 2, PADW], F32, scr_at)
        v_rows = gbuf[:, 1, :]
        prob = at("prob", [P, 2, 512], F32, scr_at)
        prob_t = at("prob_t", [P, 2, 512], F32, scr_at + size([P, 2, 512]))
        att2 = alias(scr_at + size([P, 4, T]), SBUF_END)
        bias = att2("bias", [P, 2, 3, NK])
        table = att2("rpb_table", [P, 2, TABLE])
        mask = att2("mask", [P, 3, NK])
        rowmax = att2("neg_max", [P, 2])
        rowsum = att2("row_sum", [P, 2])
        rowinv = att2("row_inv", [P, 2])
        inv_n = att2("inv_n", [P, NB])
        first_key = att2("first_key", [P, 4])
        poolw = at("pool_weights", [P, KP, P], F32, ada_at)
        key_col = at("key_col", [P, NK], F32, scr_at)
        key_ge = at("key_ge", [P, NK], F32, scr_at + 4 * NK)
        int_n = at("int_n", [P, NK], mybir.dt.int32, scr_at + 8 * NK)
        int_p = at("int_p", [P, 4], mybir.dt.int32, scr_at + 12 * NK)

        rg = alias(g_at, g_end)
        yh = rg("y_hi", [P, KR, SEQ], F32R)
        yl = rg("y_lo", [P, KR, SEQ], F32R)
        gate_r = [rg(f"gate_r{d}", [P, TG]) for d in range(2)]
        gate_i = [rg(f"gate_i{d}", [P, TG]) for d in range(2)]
        decay = [rg(f"decay{d}", [P, TG]) for d in range(2)]
        root = [rg(f"root{d}", [P, TG]) for d in range(2)]
        rg2 = alias(scr_at, SBUF_END)
        upad = rg2("u_padded", [P, PADW])
        conv = [rg2(f"conv{i}", [P, TG]) for i in range(2)]
        ch = [rg2(f"conv_hi{i}", [P, TG], F32R) for i in range(2)]
        cl = [rg2(f"conv_lo{i}", [P, TG], F32R) for i in range(2)]
        yf = rg2("y_f32", [P, SEQ])
        rg3 = alias(ada_at, ada_at + size([P, KD, 2 * P]))
        gel_q = rg3("gelu_square", [P, SEQ])
        gel_z = rg3("gelu_inner", [P, SEQ])
        gel = rg3("gelu", [P, 2, SEQ])

        pA = psum("pair_a", [P, 2 * 512])
        pB = psum("pair_b", [P, 2 * 512])
        pC = psum("pair_c", [P, 2 * 512])
        pR = psum("pair_r", [P, 2 * 512])
        pair = [pA, pB]

        raw_landed = [sem("raw_landed0"), sem("raw_landed1")]
        hi_done = sem("hi_done")
        split_ready = sem("split_ready")
        panel_used = sem("panel_used")
        silu_done = sem("silu_done")
        gate_up_done = sem("gate_up_done")
        g_hi_done = sem("g_hi_done")
        g_split_done = sem("g_split_done")
        resid_done = sem("resid_done")
        square_done = sem("square_done")
        sum_done = sem("sum_done")
        ss_done = sem("ss_done")
        ms_done = sem("ms_done")
        sd_done = sem("sd_done")
        rstd_done = sem("rstd_done")
        diag_done = sem("diag_done")
        rbc_done = sem("rbc_done")
        scaled_done = sem("scaled_done")
        mod_done = sem("mod_done")
        h_hi_done = sem("h_hi_done")
        h_ready = sem("h_ready")
        h_ctx_ready = sem("h_ctx_ready")
        ada_landed = sem("ada_landed")
        ada_summed = sem("ada_summed")
        ada0_summed = sem("ada0_summed")
        ada_used = sem("ada_used")
        mods_done = sem("mods_done")
        coef_done = sem("coef_done")
        rows_landed = sem("rows_landed")
        x_landed = sem("x_landed")
        ada0_landed = [sem(f"ada0_landed{i}") for i in range(4)]
        const_done = sem("const_done")
        cols_t = sem("cols_t")
        cols_done = sem("cols_done")
        xt_done = sem("xt_done")
        out_t = sem("out_t")
        out_copied = sem("out_copied")
        out_stored = sem("out_stored")
        proj_done = sem("proj_done")
        v_rows_done = sem("v_rows_done")
        v_turned = sem("v_turned")
        v_stored = sem("v_stored")
        v_loaded = sem("v_loaded")
        rpb_padded = sem("rpb_padded")
        rpb_opened = sem("rpb_opened")
        table_landed = [sem("table_landed0"), sem("table_landed1")]
        iota_done = sem("iota_done")
        mask_done = sem("mask_done")
        bias_done = sem("bias_done")
        poolw_landed = sem("poolw_landed")
        pooled_done = sem("pooled_done")
        poolmm_done = sem("poolmm_done")
        mixed_done = sem("mixed_done")
        mixed_hi = sem("mixed_hi")
        mixed_split = sem("mixed_split")
        scores_done = sem("scores_done")
        max_done = sem("max_done")
        prob_done = sem("prob_done")
        prob_scaled = sem("prob_scaled")
        turned_done = sem("turned_done")
        prob_t_done = sem("prob_t_done")
        pv_done = sem("pv_done")
        dve_step = sem("dve_step")
        act_step = sem("act_step")
        u_done = sem("u_done")
        conv_done = sem("conv_done")
        conv_hi = sem("conv_hi")
        conv_split = sem("conv_split")
        gelu_q = sem("gelu_q")
        gelu_z = sem("gelu_z")
        gelu_t = sem("gelu_t")
        gelu_done = sem("gelu_done")
        gates_done = sem("gates_done")
        decay_done = sem("decay_done")
        root_done = sem("root_done")
        scan_done = sem("scan_done")
        y_done = sem("y_done")
        y_hi_done = sem("y_hi_done")
        y_split = sem("y_split")
        final_scaled = sem("final_scaled")
        lam_exp = sem("lam_exp")
        rg_ready = sem("rg_ready")

        block = stack.enter_context(nc.Block())

        def chained(engine, done):
            count = [0]

            def link(instruction):
                instruction.then_inc(done, 1)
                count[0] += 1
                engine.wait_ge(done, count[0])

            return link

        def sums_before(q):
            return (q - ADA0) * (2 * KD)

        def ada_seen(q):
            return q - (ADA0 - 2)

        SPANS = [(0, 0, SEQ), (1, SEQ, T)]

        def norm_tiles(name):
            return (SEQ if name in X_ONLY else T) // P

        def norm_tiles_before(i):
            return sum(norm_tiles(name) for name in NORMS[:i])

        NORM_AT = {name: i for i, name in enumerate(NORMS)}
        SITE = {"dn00": 0, "dn01": 0, "about": 1, "dn10": 2, "dn11": 2, "dn20": 3, "dn21": 3,
                "rgout": 4, "dn30": 5, "dn31": 5}
        X_ONLY = ("rgout", "dn30", "dn31")
        GU_BEFORE = {(f, h): (2 * f + h) * KC for f in range(4) for h in range(2)}

        def shift_tile(site):
            return 3 * KD * site

        def u_panel(n):
            return P_RG if n == 0 else P_RG + 3 * n - 1

        def g_panel(n):
            return P_RG + 1 if n == 0 else P_RG + 3 * n + 1

        def gate_panel(n):
            return min(P_RG + 3 * (n + 1), P_RG + 3 * KR - 1)

        P_AB, P_ABOUT, P_RG, P_RGOUT = first["abin"], first["about"], first["rg"], first["rgout"]
        STEPS = [(h, j) for h in range(HEADS) for j in range(BLOCKS + 2)]

        @block.sync
        def _(sp):
            landed = [0]

            def span(start, n):
                return ds(start if isinstance(start, int) else sp.snap(start), n)

            def rows(src, r, count):
                a = 0
                while a < count:
                    t, q = divmod(r + a, P)
                    k = min(count - a, P - q)
                    sp.dma_start(rowbuf[q:q + k, t, :], src[a:a + k, :]).then_inc(rows_landed, 16)
                    landed[0] += 1
                    a += k

            xt = x[0].rearrange("(t p) n -> p t n", p=P)
            sp.dma_start(xin[:, 0:SEQ // P, :], xt).then_inc(x_landed, 16)
            sp.dma_start(xin[:, SEQ // P:T // P, :], ctx_in[0].rearrange("(t p) n -> p t n", p=P)).then_inc(x_landed, 16)
            rows(c.rearrange("b (k p) -> (b k) p", p=P), R_C, KD)
            rows(c_ctx.rearrange("(k p) -> k p", p=P), R_CC, KD)
            rows(ada_b.rearrange("l (k p) -> (l k) p", p=P), R_ADAB, 2 * MODS)
            rows(norm_g.rearrange("l s (k p) -> (l s k) p", p=P), R_NORM, 6 * KD)
            rows(final_g.rearrange("(k p) -> k p", p=P), R_FINAL, KD)
            rows(pool_scale.rearrange("o (k p) -> (o k) p", p=P), R_PSCALE, KP)
            rows(conv_w.rearrange("o w (k p) -> (o w k) p", p=P), R_CONVW, CONV * KR)
            rows(conv_b.rearrange("o (k p) -> (o k) p", p=P), R_CONVB, KR)
            rows(gate_b.rearrange("o d g (k p) -> (o d g k) p", p=P), R_GATEB, 4 * KR)
            rows(lam.rearrange("o d (k p) -> (o d k) p", p=P), R_LAM, 2 * KR)
            assert landed[0] == ROW_DMAS, landed[0]
            w0 = ada_w[0].rearrange("(k p) n -> p k n", p=P)
            for i in range(4):
                chunk = slice(i * ADA0_W, (i + 1) * ADA0_W)
                sp.dma_start(ada0[:, :, chunk], w0[:, :, chunk]).then_inc(ada0_landed[i], 16)

            def load(p, par, kt, src):
                if not isinstance(p, int) or p >= 2:
                    sp.wait_ge(split_ready, p - 1)
                sp.dma_start(raw[:, par, 0:kt * P].rearrange("p (k n) -> p k n", n=P), src).then_inc(raw_landed[par], 16)

            def load_ada(q, col, layer):
                w = ada_w[layer].rearrange("(k p) n -> p k n", p=P)[:, :, span(col * (2 * P), 2 * P)]
                if not isinstance(q, int) or q > ADA0:
                    sp.wait_ge(ada_summed, sums_before(q))
                sp.dma_start(ada_raw[:, :, :], w).then_inc(ada_landed, 16)

            def with_ada(q0, start, count, body):
                cuts = [start, count]
                if q0 is not None and q0 + start < MODS // 2 < q0 + count:
                    cuts = [start, MODS // 2 - q0, count]
                for a, b in zip(cuts, cuts[1:]):
                    with sp.Fori(a, b) as i:
                        layer = ((q0 or 0) + a) // (MODS // 2)
                        body(i, lambda: q0 is not None and load_ada(i + q0, i + (q0 - layer * (MODS // 2)), layer))

            def ffn(f):
                layer, which = divmod(f, 2)
                gu = w_gu[layer, which].rearrange("(k p) n -> p k n", p=P)
                dn = w_down[layer, which].rearrange("(k p) n -> p k n", p=P)
                for h in range(2):
                    p0 = first[f"gu{f}{h}"]

                    def gate_up(i, between):
                        load(i * 2 + p0, 0, KD, gu[:, :, span(i * P + h * KC * P, P)])
                        between()
                        load(i * 2 + (p0 + 1), 1, KD, gu[:, :, span(i * P + (DFF + h * KC * P), P)])

                    if p0 == 0:
                        load(0, 0, KD, gu[:, :, 0:P])
                        load(1, 1, KD, gu[:, :, DFF:DFF + P])
                        load_ada(ADA0, ADA0, 0)
                        pad_rpb()
                    with_ada(ada_first.get(f"gu{f}{h}"), int(p0 == 0), KC, gate_up)
                    p0 = first[f"dn{f}{h}"]

                    def down(i, between):
                        for r in range(2):
                            load(i * 2 + (p0 + r), r, KC, dn[:, h * KC:(h + 1) * KC, span(i * (2 * P) + r * P, P)])
                            if r == 0:
                                between()

                    with_ada(ada_first.get(f"dn{f}{h}"), 0, KD // 2, down)

            def pad_rpb():
                flat = rpb.rearrange("o h r c -> o (h r c)")
                n = HEADS * RPB_R * RPB_C
                sp.dma_start(rpb_pad[:, 16:16 + n], flat).then_inc(rpb_padded, 16)
                sp.dma_start(rpb_pad[:, 0:16], flat[:, 0:16]).then_inc(rpb_padded, 16)
                sp.dma_start(rpb_pad[:, 16 + n:32 + n], flat[:, 0:16]).then_inc(rpb_padded, 16)

            def open_rpb():
                sp.wait_ge(rpb_padded, 48)
                for h in range(HEADS):
                    src = bass.AP(tensor=rpb_pad.tensor, offset=h * RPB_R * RPB_C, ap=[[1, NB], [RPB_C, GRID_R], [1, TABLE]])
                    sp.dma_start(rpb_open[h].rearrange("(c r) n -> c r n", r=GRID_R), src).then_inc(rpb_opened, 16)

            ffn(0)

            win = ab_in[0].rearrange("(k p) n -> p k n", p=P)
            order = [0, 3, 2, 1]
            for n in range(4):
                if n == 1:
                    sp.wait_ge(ada_used, ada_seen(ada_first["gu10"] - 1))
                    sp.dma_start(poolw[:, :, :], pool_w[0].rearrange("g k j -> k g j")).then_inc(poolw_landed, 16)
                    open_rpb()
                with sp.Fori(0, 2) as i:
                    for r in range(2):
                        load(i * 2 + (P_AB + 4 * n + r), r, KD, win[:, :, span(i * (2 * P) + (order[n] * KP + r) * P, P)])
            sp.wait_ge(proj_done, 2 + 8)
            vc = v_cols.rearrange("(c r) n -> r c n", r=GRID_R)
            for r in range(GRID_R):
                sp.dma_start(vc[r], vtok[GRID_W * (r % 2):GRID_W * (r % 2 + 1), r // 2, :]).then_inc(v_stored, 16)
            sp.wait_ge(v_stored, 16 * GRID_R)
            for j in range(BLOCKS):
                src = v_cols[SLAB_AT[j] * GRID_R:SLAB_AT[j] * GRID_R + NK, :].rearrange("(t p) n -> p t n", p=P)
                sp.dma_start(vslab[:, 2 * j:2 * j + 2, :], src).then_inc(v_loaded, 16)
            wout = ab_out[0].rearrange("(k p) n -> p k n", p=P)
            sp.wait_ge(rpb_opened, 16 * HEADS)
            for h in range(HEADS):
                if h >= 2:
                    sp.wait_ge(bias_done, h - 1)
                sp.dma_start(table[:, h % 2, :], rpb_open[h]).then_inc(table_landed[h % 2], 16)
                if h == 1:
                    for r in range(2):
                        load(P_ABOUT + r, r, KD, wout[:, :, r * P:(r + 1) * P])
            with sp.Fori(1, KD // 2) as i:
                for r in range(2):
                    load(i * 2 + (P_ABOUT + r), r, KD, wout[:, :, span(i * (2 * P) + r * P, P)])

            ffn(1)
            ffn(2)

            rin = rg_in[0].rearrange("(k p) n -> p k n", p=P)
            gw = gate_w[0].rearrange("d g n k j -> n k (d g) j")
            DR = KR * P

            def load_u(p, par, n):
                load(p, par, KD, rin[:, :, span(n * P + DR, P)])

            def load_g(p, par, n):
                src = rin[:, :, 0:P] if isinstance(n, int) and n == 0 else rin[:, :, P:DR][:, :, ds((n - 1) * P, P)]
                load(p, par, KD, src)

            def load_gates(p, par, n):
                src = gw[ds(n, 1)].rearrange("o k b j -> (o k) b j")
                load(p, par, 4, src)

            load_u(P_RG, 0, 0)
            load_g(P_RG + 1, 1, 0)
            with sp.Fori(0, KR // 2 - 1) as i:
                for b in range(2):
                    p = i * 6 + (P_RG + 2 + 3 * b)
                    load_u(p, b, i * 2 + (b + 1))
                    load_gates(p + 1, 1 - b, i * 2 + b)
                    load_g(p + 2, b, i * 2 + (b + 1))
            p = P_RG + 3 * KR - 4
            load_u(p, 0, KR - 1)
            load_gates(p + 1, 1, KR - 2)
            load_g(p + 2, 0, KR - 1)
            load_gates(p + 3, 1, KR - 1)
            wro = rg_out[0].rearrange("(k p) n -> p k n", p=P)
            with sp.Fori(0, KD // 2) as i:
                for r in range(2):
                    load(i * 2 + (P_RGOUT + r), r, KR, wro[:, :, span(i * (2 * P) + r * P, P)])

            ffn(3)
            for half in range(2):
                sp.wait_ge(out_copied, KD // 2 * (half + 1))
                n0 = half * (D // 2)
                sp.dma_start(out[0].rearrange("(t p) n -> p t n", p=P)[:, :, n0:n0 + D // 2],
                             xin[:, 0:SEQ // P, n0:n0 + D // 2]).then_inc(out_stored, 16)
            sp.wait_ge(out_stored, 32)

        @block.gpsimd
        def _(pool):
            nc.gpsimd.memset(ident[:, :], 0.0).then_inc(const_done, 1)
            nc.gpsimd.memset(ones[:, :], 1.0).then_inc(const_done, 1)
            pool.wait_ge(const_done, 1)
            nc.gpsimd.affine_select(out=ident[:, :], in_=ident[:, :], compare_op=ALU.not_equal, fill=1.0, base=0,
                                    pattern=[[-1, P]], channel_multiplier=1).then_inc(const_done, 1)

            def low(p, par, kt):
                pool.wait_ge(hi_done, p + 1)
                nc.gpsimd.tensor_tensor(wl[:, par, 0:kt * P], raw[:, par, 0:kt * P],
                                        wh[:, par, 0:kt * P].bitcast(F32), ALU.subtract).then_inc(split_ready, 1)

            def pairs(p0, start, count, kt):
                with pool.Fori(start, count) as i:
                    for r in range(2):
                        low(i * 2 + (p0 + r), r, kt)

            def norm(name):
                i = NORM_AT[name]
                for k in range(KD):
                    pool.wait_ge(h_hi_done, i * KD + k + 1)
                    nc.gpsimd.tensor_tensor(hl[:, k, 0:SEQ], normed[k % 4][:, 0:SEQ], hh[:, k, 0:SEQ].bitcast(F32),
                                            ALU.subtract).then_inc(h_ready, 1)

            def ffn(f, after):
                low(first[f"gu{f}0"], 0, KD)
                low(first[f"gu{f}0"] + 1, 1, KD)
                norm(after)
                pairs(first[f"gu{f}0"], 1, KC, KD)
                pairs(first[f"dn{f}0"], 0, KD // 2, KC)
                pairs(first[f"gu{f}1"], 0, KC, KD)
                pairs(first[f"dn{f}1"], 0, KD // 2, KC)

            ffn(0, "in")
            low(P_AB, 0, KD)
            low(P_AB + 1, 1, KD)
            norm("dn01")
            pool.wait_ge(h_ready, (NORM_AT["dn01"] + 1) * KD)
            nc.gpsimd.iota(int_n[:, :], [[1, SLAB], [0, GRID_R]], base=0, channel_multiplier=0).then_inc(iota_done, 1)
            nc.gpsimd.iota(int_p[:, 0:1], [[0, 1]], base=0, channel_multiplier=1).then_inc(iota_done, 1)
            pairs(P_AB, 1, 8, KD)
            for h in range(HEADS):
                if h == 2:
                    low(P_ABOUT, 0, KD)
                    low(P_ABOUT + 1, 1, KD)
                pool.wait_ge(table_landed[h % 2], 16 * (h // 2 + 1))
                pool.wait_ge(mask_done, 1)
                if h >= 2:
                    pool.wait_ge(scores_done, (BLOCKS + 2) * (h - 2) + BLOCKS)
                for v in range(3):
                    t = bass.AP(tensor=table[:, :, :].tensor, offset=table[:, h % 2, SHIFT[v]:SHIFT[v] + 1].offset,
                                ap=[list(table[:, 0, 0:1].ap[0]), [1, SLAB], [RPB_C, GRID_R]])
                    last = nc.gpsimd.tensor_tensor(bias[:, h % 2, v, :].rearrange("p (c r) -> p c r", r=GRID_R), t,
                                                   mask[:, v, :].rearrange("p (c r) -> p c r", r=GRID_R), ALU.add)
                last.then_inc(bias_done, 1)
            pairs(P_ABOUT, 1, KD // 2, KD)
            ffn(1, "about")
            ffn(2, "dn11")
            low(P_RG, 0, KD)
            low(P_RG + 1, 1, KD)
            norm("dn21")

            def conv_low(n):
                pool.wait_ge(conv_hi, n + 1)
                nc.gpsimd.tensor_tensor(cl[n % 2][:, :], conv[n % 2][:, :], ch[n % 2][:, :].bitcast(F32),
                                        ALU.subtract).then_inc(conv_split, 1)

            def y_low(n):
                pool.wait_ge(y_hi_done, n + 1)
                nc.gpsimd.tensor_tensor(yl[:, n, :], yf[:, :], yh[:, n, :].bitcast(F32),
                                        ALU.subtract).then_inc(y_split, 1)

            for n in range(1, KR):
                p = P_RG + 3 * n - 1
                low(p, (n + 1) % 2, KD)
                low(p + 1, n % 2, 4)
                if n == 1:
                    conv_low(0)
                low(p + 2, (n + 1) % 2, KD)
                if n >= 2:
                    y_low(n - 2)
                conv_low(n)
            low(P_RG + 3 * KR - 1, 1, 4)
            y_low(KR - 2)
            low(P_RGOUT, 0, KR)
            low(P_RGOUT + 1, 1, KR)
            y_low(KR - 1)
            pairs(P_RGOUT, 1, KD // 2, KR)
            ffn(3, "rgout")

        @block.scalar
        def _(act):
            chain = chained(act, act_step)

            def high(p, par=None):
                kt = KD
                if isinstance(p, int):
                    if p >= NPANELS:
                        return
                    par, kt = p % 2, ktiles[p]
                    land = 16 * (p // 2 + 1)
                    if p >= 2:
                        act.wait_ge(panel_used, p - 1)
                    act.wait_ge(raw_landed[par], land)
                nc.scalar.activation(wh[:, par, 0:kt * P], raw[:, par, 0:kt * P], ACT.Copy).then_inc(hi_done, 1)

            def silu(F, p):
                act.wait_ge(panel_used, p + 1)
                act.wait_ge(gate_up_done, F + 1)
                if f_width[0] == T:
                    nc.scalar.activation(sbuf[:, 0, :], pA[:, 0:T], ACT.Silu).then_inc(silu_done, 1)
                else:
                    nc.scalar.activation(sbuf[:, 0, 0:SEQ], pA[:, 0:SEQ], ACT.Silu).then_inc(silu_done, 1)

            f_width = [T]

            def gate_up(f, h):
                f_width[0] = SEQ if f == 3 else T
                p0, F0 = first[f"gu{f}{h}"], GU_BEFORE[f, h]
                with act.Fori(0, KC - 1) as i:
                    silu(i + F0, i * 2 + p0)
                    for r in range(2):
                        act.wait_ge(panel_used, i * 2 + (p0 + r + 1))
                        act.wait_ge(raw_landed[r], i * 16 + 16 * ((p0 + r) // 2 + 2))
                        high(None, r)
                silu(KC - 1 + F0, 2 * (KC - 1) + p0)
                high(p0 + 2 * KC)
                high(p0 + 2 * KC + 1)

            def square(name, k):
                i = NORM_AT[name]
                W = SEQ if name in X_ONLY else T
                act.wait_ge(resid_done, UPD[name] + k + 1)
                if k >= 3:
                    act.wait_ge(sum_done, i * (KD - 1) + k - 2)
                dst = acc if k == 0 else sbuf[:, k % 2, :]
                nc.scalar.activation(dst[:, 0:W], resid[:, k, 0:W], ACT.Square).then_inc(square_done, 1)

            def norm(name):
                i = NORM_AT[name]
                W = SEQ if name in X_ONLY else T
                n = W // P
                act.wait_ge(ms_done, i + 1)
                nc.scalar.activation(sd[:, 0:n], ms[:, 0:n], ACT.Sqrt).then_inc(sd_done, 1)
                if name == "dn31":
                    for k in range(KD):
                        act.wait_ge(scaled_done, i * KD + k + 1)
                        if k >= 2:
                            act.wait_ge(out_t, k - 1)
                        nc.scalar.activation(gbuf[:, k % 2, 0:SEQ], sbuf[:, k % 2, 0:SEQ], ACT.Copy,
                                             scale=cols[:, R_FINAL + k:R_FINAL + k + 1]).then_inc(final_scaled, 1)
                    return
                site = i
                if name == "in":
                    high(0)
                    high(1)
                act.wait_ge(coef_done, 3 * site + 2)
                for k in range(KD):
                    act.wait_ge(scaled_done, i * KD + k + 1)
                    t = shift_tile(site) + k
                    rows = normed[k % 4]
                    nc.scalar.activation(rows[:, 0:SEQ], rows[:, 0:SEQ], ACT.Identity, bias=mods[:, t, 0:1])\
                        .then_inc(mod_done, 1)
                    if W == T:
                        nc.scalar.activation(hh[:, k, SEQ:T], rows[:, SEQ:T], ACT.Identity, bias=mods[:, t, 1:2])
                    act.wait_ge(mod_done, i * KD + k + 1)
                    nc.scalar.activation(hh[:, k, 0:SEQ], rows[:, 0:SEQ], ACT.Copy).then_inc(h_hi_done, 1)

            def copy_turned(s):
                j, b = STEPS[s][1], s % 2
                W = NK + CTX if j < BLOCKS else CTX
                act.wait_ge(turned_done, s + 1)
                if s >= 2:
                    act.wait_ge(pv_done, s - 1)
                nc.scalar.activation(prob_t[:, b, 0:W], pB[:, b * 512:b * 512 + W], ACT.Copy).then_inc(prob_t_done, 1)

            def outputs(name, p0):
                if name in NORM_AT:
                    chain(nc.scalar.activation(sd[:, 7:8], ones[:, 0:1], ACT.Sqrt))
                for k in range(KD):
                    high(p0 + k + 2)
                    if name in NORM_AT:
                        square(name, k)

            def ffn(f):
                for h in range(2):
                    gate_up(f, h)
                    outputs(f"dn{f}{h}", first[f"dn{f}{h}"])
                norm(f"dn{f}1")

            act.wait_ge(cols_done, 1)
            for v, r in ((0, R_C), (1, R_CC)):
                last = nc.scalar.activation(cvec[:, :, v], cols[:, r:r + KD], ACT.Silu)
            last.then_inc(silu_done, 1)
            act.wait_ge(const_done, 3)
            chain(nc.scalar.activation(sd[:, 7:8], ones[:, 0:1], ACT.Sqrt))
            for k in range(KD):
                square("in", k)
            norm("in")
            act.wait_ge(lam_exp, 1)
            nc.scalar.activation(lam_s[:, 1, :], lam_s[:, 0, :], ACT.Exp, scale=-1.0).then_inc(lam_exp, 1)
            ffn(0)

            for j in range(16):
                high(P_AB + j + 2)
            for g in range(KP):
                act.wait_ge(poolmm_done, g + 1)
                act.wait_ge(v_stored, 16 * GRID_R)
                if g >= 2:
                    act.wait_ge(mixed_split, g - 1)
                ps = pC if g % 2 == 0 else pR
                nc.scalar.activation(att_f[:, g % 2, :], ps[:, 0:T], ACT.Copy,
                                     scale=cols[:, R_PSCALE + g:R_PSCALE + g + 1]).then_inc(mixed_done, 1)
                act.wait_ge(mixed_done, g + 1)
                nc.scalar.activation(hh[:, g, :], att_f[:, g % 2, :], ACT.Copy).then_inc(mixed_hi, 1)
            for s, (h, j) in enumerate(STEPS):
                W = NK + CTX if j < BLOCKS else CTX
                b = s % 2
                act.wait_ge(max_done, s + 1)
                if s >= 2:
                    act.wait_ge(turned_done, s - 1)
                nc.scalar.activation(prob[:, b, 0:W], pA[:, b * 512:b * 512 + W], ACT.Exp, bias=rowmax[:, b:b + 1],
                                     accum_out=rowsum[:, b:b + 1]).then_inc(prob_done, 1)
                if s >= 1:
                    copy_turned(s - 1)
            copy_turned(len(STEPS) - 1)
            outputs("about", P_ABOUT)
            norm("about")
            ffn(1)
            ffn(2)

            def u_rows(n):
                act.wait_ge(panel_used, u_panel(n) + 1)
                if n == 0:
                    act.wait_ge(rg_ready, 1)
                else:
                    act.wait_ge(conv_done, n)
                nc.scalar.activation(upad[:, PAD_X:PAD_X + SEQ], pA[:, 0:SEQ], ACT.Copy)
                nc.scalar.activation(upad[:, PAD_C:PAD_C + CTX], pA[:, 512:512 + CTX], ACT.Copy).then_inc(u_done, 1)

            def gelu_rows(n):
                act.wait_ge(panel_used, g_panel(n) + 1)
                if n >= 1:
                    act.wait_ge(gelu_done, n)
                nc.scalar.activation(gel_q[:, :], pB[:, 0:SEQ], ACT.Square, scale=0.044715 ** 0.5).then_inc(gelu_q, 1)

            def gelu_tanh(n):
                act.wait_ge(gelu_z, n + 1)
                nc.scalar.activation(gel_q[:, :], gel_z[:, :], ACT.Tanh, scale=(2 / 3.141592653589793) ** 0.5)\
                    .then_inc(gelu_t, 1)

            def gates(n):
                act.wait_ge(panel_used, gate_panel(n) + 1)
                if n == 0:
                    act.wait_ge(rg_ready, 2)
                else:
                    act.wait_ge(decay_done, 2 * n)
                for g, dst in enumerate((gate_r, gate_i)):
                    for d in range(2):
                        xp, x0 = ((pB, 512), (pC, 0), (pR, 0), (pR, 512))[2 * d + g]
                        cc, c0 = (pC, 512) if d == 0 else (pA, 512)
                        half = half_gb[:, (2 * d + g) * KR + n:(2 * d + g) * KR + n + 1]
                        if g == 1 and n >= 1:
                            act.wait_ge(scan_done, 2 * (n - 1) + d + 1)
                        nc.scalar.activation(dst[d][:, 0:SEQ], xp[:, x0:x0 + SEQ], ACT.Tanh, bias=half, scale=0.5)
                        nc.scalar.activation(dst[d][:, GAP_C:TG], cc[:, c0 + g * CTX:c0 + (g + 1) * CTX], ACT.Tanh,
                                             bias=half, scale=0.5).then_inc(gates_done, 1)
                act.wait_ge(gates_done, 4 * n + 2)
                if n >= 1:
                    act.wait_ge(y_done, n)
                for d in range(2):
                    m = d * KR + n
                    nc.scalar.activation(decay[d][:, :], gate_r[d][:, :], ACT.Exp, bias=rg_scale[:, m:m + 1],
                                         scale=rg_scale[:, m:m + 1])
                    nc.scalar.activation(root[d][:, :], gate_r[d][:, :], ACT.Tanh, bias=rg_tanh[:, m:m + 1],
                                         scale=rg_tanh[:, m:m + 1]).then_inc(decay_done, 1)
                for d in range(2):
                    act.wait_ge(decay_done, 2 * n + d + 1)
                    nc.scalar.activation(root[d][:, :], root[d][:, :], ACT.Sqrt, scale=0.25).then_inc(root_done, 1)

            high(P_RG + 2)
            u_rows(0)
            high(P_RG + 3)
            gelu_rows(0)
            for n in range(1, KR):
                high(P_RG + 3 * n + 1)
                u_rows(n)
                gelu_tanh(n - 1)
                high(P_RG + 3 * n + 2)
                gates(n - 1)
                high(P_RG + 3 * n + 3)
                gelu_rows(n)
            high(P_RG + 3 * KR + 1)
            gelu_tanh(KR - 1)
            gates(KR - 1)
            outputs("rgout", P_RGOUT)
            norm("rgout")
            ffn(3)

        @block.vector
        def _(dve):
            chain = chained(dve, dve_step)

            def coef_a(site):
                layer, j = divmod(site, 3)
                t = shift_tile(site) + KD
                r = R_NORM + (layer * 3 + j) * KD
                for v in range(2):
                    nc.vector.scalar_tensor_tensor(out=mod_a[:, site, :, v], in0=mods[:, t:t + KD, v], scalar=1.0,
                                                   in1=cols[:, r:r + KD], op0=ALU.add, op1=ALU.mult)\
                        .then_inc(coef_done, 1)

            def coef_g(site):
                t = shift_tile(site) + 2 * KD
                nc.vector.tensor_scalar(mod_g[:, site, :, :], mods[:, t:t + KD, :], 1.0 if site % 3 == 1 else 0.5, None,
                                        ALU.mult).then_inc(coef_done, 1)

            def sum_tiles(tiles, sums, signal, before):
                for k in range(KD):
                    for v in range(2):
                        n = 2 * k + v
                        c_k = cvec[:, k, v:v + 1]
                        if k == 0:
                            step = nc.vector.tensor_scalar(sums[v], tiles(k), c_k, None, ALU.mult)
                        else:
                            dve.wait_ge(signal, before + (n - 1))
                            step = nc.vector.scalar_tensor_tensor(out=sums[v], in0=tiles(k), scalar=c_k, in1=sums[v],
                                                                  op0=ALU.mult, op1=ALU.add)
                        step.then_inc(signal, 1)

            def sum_ada(q):
                dve.wait_ge(ada_landed, (q - (ADA0 - 1)) * 16)
                sum_tiles(lambda k: ada_raw[:, k, :], [ada_sum[:, v, :] for v in range(2)], ada_summed, sums_before(q))

            def take_ada(q):
                dve.wait_ge(ada_used, q - (ADA0 - 2))
                src = pC[:, 0:4].rearrange("p (t v) -> p v t", v=2)
                for v in range(2):
                    last = nc.vector.tensor_tensor(mods[:, ds(q * 2, 2), v], src[:, v, :], cols[:, ds(q * 2, 2)], ALU.add)
                last.then_inc(mods_done, 1)

            def gate_up(f, h):
                W = SEQ if f == 3 else T
                p0, F0 = first[f"gu{f}{h}"], GU_BEFORE[f, h]
                q0 = ada_first.get(f"gu{f}{h}")
                with dve.Fori(0, KC) as i:
                    if q0 is not None:
                        sum_ada(i + q0)
                    dve.wait_ge(silu_done, i + (F0 + 2))
                    dve.wait_ge(panel_used, i * 2 + (p0 + 2))
                    dve.wait_ge(g_split_done, i + (F0 + 1))
                    nc.vector.tensor_tensor(gbuf[:, 0, 0:W], sbuf[:, 0, 0:W], pB[:, 0:W], ALU.mult)\
                        .then_inc(gate_up_done, 1)
                    dve.wait_ge(gate_up_done, i + (F0 + 2))
                    nc.vector.tensor_copy(gh[:, ds(i, 1), 0:W].rearrange("p o n -> p (o n)"), gbuf[:, 0, 0:W])\
                        .then_inc(g_hi_done, 1)
                    dve.wait_ge(g_hi_done, i + (F0 + 1))
                    nc.vector.tensor_tensor(gl[:, ds(i, 1), 0:W].rearrange("p o n -> p (o n)"), gbuf[:, 0, 0:W],
                                            gh[:, ds(i, 1), 0:W].rearrange("p o n -> p (o n)").bitcast(F32),
                                            ALU.subtract).then_inc(g_split_done, 1)
                    if q0 is not None:
                        take_ada(i + q0)

            def add_square(name, k):
                i = NORM_AT[name]
                W = SEQ if name in X_ONLY else T
                dve.wait_ge(square_done, i * KD + k + 1)
                if k >= 2:
                    dve.wait_ge(sum_done, i * (KD - 1) + k - 1)
                nc.vector.tensor_tensor(acc[:, 0:W], acc[:, 0:W], sbuf[:, k % 2, 0:W], ALU.add).then_inc(sum_done, 1)

            def outputs(name, p0):
                site = SITE[name]
                if name[:2] != "dn" or name[3] == "0":
                    dve.wait_ge(mods_done, ada_seen((shift_tile(site) + 3 * KD) // 2 - 1))
                    coef_g(site)
                    dve.wait_ge(coef_done, 3 * site + 3)
                q0 = ada_first.get(name)
                for k in range(KD):
                    if q0 is not None:
                        if k % 2 == 0:
                            sum_ada(q0 + k // 2)
                        else:
                            take_ada(q0 + k // 2)
                    dve.wait_ge(panel_used, p0 + k + 1)
                    ps = pair[k % 2]
                    last = nc.vector.scalar_tensor_tensor(out=resid[:, k, 0:SEQ], in0=ps[:, 0:SEQ],
                                                          scalar=mod_g[:, site, k, 0:1], in1=resid[:, k, 0:SEQ],
                                                          op0=ALU.mult, op1=ALU.add)
                    if name not in X_ONLY:
                        last = nc.vector.scalar_tensor_tensor(out=resid[:, k, SEQ:T], in0=ps[:, 512:512 + CTX],
                                                              scalar=mod_g[:, site, k, 1:2], in1=resid[:, k, SEQ:T],
                                                              op0=ALU.mult, op1=ALU.add)
                    last.then_inc(resid_done, 1)
                    if name in NORM_AT and k >= 2:
                        add_square(name, k - 1)
                if name in NORM_AT:
                    add_square(name, KD - 1)

            def norm(name):
                i = NORM_AT[name]
                W = SEQ if name in X_ONLY or name == "dn31" else T
                n = W // P
                if name not in ("in", "dn31"):
                    dve.wait_ge(mods_done, ada_seen((shift_tile(i) + 2 * KD) // 2 - 1))
                    coef_a(i)
                dve.wait_ge(ss_done, i + 1)
                nc.vector.tensor_scalar(ms[:, 0:n], pC[:, 512:512 + n], 1.0 / D, EPS, ALU.mult, ALU.add)\
                    .then_inc(ms_done, 1)
                dve.wait_ge(sd_done, i + 1)
                nc.vector.reciprocal(rstd[:, 0:n], sd[:, 0:n]).then_inc(rstd_done, 1)
                dve.wait_ge(rstd_done, i + 1)
                for t in range(n):
                    nc.vector.tensor_scalar(acc[:, t * P:(t + 1) * P], ident[:, :], rstd[:, t:t + 1], None,
                                            ALU.mult).then_inc(diag_done, 1)
                if name == "dn01":
                    nc.vector.memset(pT[:, :, 0:PAD_X], 0.0)
                    nc.vector.memset(pT[:, :, PADW - 8:PADW], 0.0).then_inc(proj_done, 1)
                    nc.vector.memset(pT[:, :, PAD_X + SEQ:PAD_C], 0.0).then_inc(proj_done, 1)
                if name == "in":
                    first_ada()
                    coef_a(i)
                if name != "dn31":
                    dve.wait_ge(coef_done, 3 * i + 2)
                    for k in range(KD):
                        if k >= 4:
                            dve.wait_ge(h_ready, i * KD + k - 3)
                        for v, a, b in SPANS[:1 if W == SEQ else 2]:
                            if k == 0:
                                dve.wait_ge(rbc_done, norm_tiles_before(i) + b // P)
                            last = nc.vector.scalar_tensor_tensor(out=normed[k % 4][:, a:b], in0=resid[:, k, a:b],
                                                                  scalar=mod_a[:, i, k, v:v + 1], in1=pR[:, a:b],
                                                                  op0=ALU.mult, op1=ALU.mult)
                        last.then_inc(scaled_done, 1)
                        if W == T and k >= 1:
                            context_low(i, k - 1)
                    if W == T:
                        context_low(i, KD - 1)
                    return
                dve.wait_ge(rbc_done, norm_tiles_before(i) + n)
                for k in range(KD):
                    if k >= 2:
                        dve.wait_ge(final_scaled, k - 1)
                    nc.vector.tensor_tensor(sbuf[:, k % 2, 0:W], resid[:, k, 0:W], pR[:, 0:W], ALU.mult)\
                        .then_inc(scaled_done, 1)
                    if k >= 1:
                        copy_out(k - 1)
                copy_out(KD - 1)

            def context_low(i, k):
                dve.wait_ge(h_hi_done, i * KD + k + 1)
                nc.vector.scalar_tensor_tensor(out=hl[:, k, SEQ:T], in0=normed[k % 4][:, SEQ:T],
                                               scalar=mods[:, shift_tile(i) + k, 1:2],
                                               in1=hh[:, k, SEQ:T].bitcast(F32), op0=ALU.add, op1=ALU.subtract)\
                    .then_inc(h_ctx_ready, 1)

            def first_ada():
                dve.wait_ge(silu_done, 1)
                for half in range(2):
                    dve.wait_ge(ada0_landed[2 + half], 16)
                    c0 = (2 + half) * ADA0_W
                    sum_tiles(lambda k: ada0[:, k, c0:c0 + ADA0_W], [ada0_sum[:, half, v, :] for v in range(2)],
                              ada0_summed, 2 * KD * half)
                dve.wait_ge(ada_used, 1)
                src = pC[:, 0:4 * ADA0].rearrange("p (t v) -> p v t", v=2)
                for v in range(2):
                    last = nc.vector.tensor_tensor(mods[:, 0:2 * ADA0, v], src[:, v, :], cols[:, 0:2 * ADA0], ALU.add)
                last.then_inc(mods_done, 1)
                dve.wait_ge(mods_done, 1)

            def copy_out(k):
                dve.wait_ge(out_t, k + 1)
                nc.vector.tensor_copy(xin[:, 0:SEQ // P, k * P:(k + 1) * P],
                                      pair[k % 2][:, 0:SEQ].rearrange("p (t n) -> p t n", n=P)).then_inc(out_copied, 1)

            def ffn(f):
                for h in range(2):
                    gate_up(f, h)
                    outputs(f"dn{f}{h}", first[f"dn{f}{h}"])
                norm(f"dn{f}1")

            dve.wait_ge(cols_t, 1)
            nc.vector.tensor_copy(cols[:, :], pR[:, 0:ROWS]).then_inc(cols_done, 1)
            dve.wait_ge(cols_done, 1)
            nc.vector.tensor_scalar(half_gb[:, :], cols[:, R_GATEB:R_GATEB + 4 * KR], 0.5, None, ALU.mult)\
                .then_inc(gate_up_done, 1)
            nc.vector.tensor_scalar(lam_s[:, 2, :], cols[:, R_LAM:R_LAM + 2 * KR], -1.0, None, ALU.mult)\
                .then_inc(g_split_done, 1)
            dve.wait_ge(g_split_done, 1)
            nc.vector.tensor_tensor(lam_s[:, 0, :], cols[:, R_LAM:R_LAM + 2 * KR], lam_s[:, 2, :], ALU.max)\
                .then_inc(lam_exp, 1)
            for k in range(KD):
                dve.wait_ge(xt_done, k + 1)
                nc.vector.tensor_copy(resid[:, k, :], pair[k % 2][:, 0:T]).then_inc(resid_done, 1)
                if k >= 2:
                    add_square("in", k - 1)
            add_square("in", KD - 1)
            norm("in")
            dve.wait_ge(lam_exp, 2)
            e, z, w = lam_s[:, 1, :], lam_s[:, 3, :], lam_s[:, 0, :]
            chain(nc.vector.tensor_scalar(z, e, 2.0, None, ALU.add))
            chain(nc.vector.reciprocal(w, z))
            chain(nc.vector.tensor_tensor(z, e, w, ALU.mult))
            chain(nc.vector.tensor_tensor(w, z, z, ALU.mult))
            chain(nc.vector.tensor_scalar(e, w, 1.0 / 19, None, ALU.mult))
            for m in range(17, 1, -2):
                chain(nc.vector.scalar_tensor_tensor(out=e, in0=e, scalar=1.0 / m, in1=w, op0=ALU.add, op1=ALU.mult))
            chain(nc.vector.scalar_tensor_tensor(out=e, in0=e, scalar=1.0, in1=z, op0=ALU.add, op1=ALU.mult))
            chain(nc.vector.tensor_scalar(w, lam_s[:, 2, :], 0.0, None, ALU.max))
            chain(nc.vector.scalar_tensor_tensor(out=w, in0=e, scalar=2.0, in1=w, op0=ALU.mult, op1=ALU.add))
            chain(nc.vector.tensor_scalar(rg_scale[:, :], w, -RG_C / 2, None, ALU.mult))
            chain(nc.vector.tensor_scalar(rg_tanh[:, :], w, RG_C / 4, None, ALU.mult))
            ffn(0)


            def column_major(ps):
                return ps[:, 0:SEQ].rearrange("p (r c) -> p c r", c=GRID_W)

            def take_values(m):
                dve.wait_ge(v_turned, m + 1)
                ps = pC if m % 2 == 0 else pR
                nc.vector.tensor_copy(vtok[:, :, m * P:(m + 1) * P], ps[:, 0:T].rearrange("p (t n) -> p t n", n=P))\
                    .then_inc(proj_done, 1)

            def project(j):
                n, m = divmod(j, KP)
                ps = pair[j % 2]
                if j == 2 * KP:
                    take_values(KP - 1)
                dve.wait_ge(panel_used, P_AB + j + 1)
                if n == 1:
                    if m >= 1:
                        dve.wait_ge(v_turned, m)
                    nc.vector.tensor_copy(v_rows, ps[:, 0:T]).then_inc(v_rows_done, 1)
                    if m >= 1:
                        take_values(m - 1)
                    return
                if n == 0:
                    nc.vector.tensor_copy(pT[:, m, PAD_X:PAD_X + SEQ], ps[:, 0:SEQ])
                    last = nc.vector.tensor_copy(pT[:, m, PAD_C:PAD_C + CTX], ps[:, 512:512 + CTX])
                else:
                    dst, scale = (kT, 1.0) if n == 2 else (qT, DH ** -0.5)
                    to = dst[:, m, 0:SEQ] if n == 2 else dst[:, m, 0:SEQ][:, ::-1]
                    nc.vector.tensor_scalar(to.rearrange("p (c r) -> p c r", r=GRID_R), column_major(ps),
                                            scale, None, ALU.mult)
                    last = nc.vector.tensor_scalar(dst[:, m, SEQ:T], ps[:, 512:512 + CTX], scale, None, ALU.mult)
                last.then_inc(proj_done, 1)

            def masks():
                dve.wait_ge(iota_done, 2)
                chain(nc.vector.tensor_scalar(int_p[:, 1:2], int_p[:, 0:1], 3, None, ALU.arith_shift_right))
                chain(nc.vector.tensor_copy(first_key[:, 3:4], int_p[:, 1:2]))
                chain(nc.vector.tensor_scalar(first_key[:, 1:2], first_key[:, 3:4], -1.0, NB - 1.0, ALU.mult, ALU.add))
                chain(nc.vector.tensor_copy(key_col[:, :], int_n[:, :]))
                chain(nc.vector.tensor_scalar(first_key[:, 0:1], first_key[:, 1:2], -8.0, 0.0, ALU.add, ALU.max))
                chain(nc.vector.tensor_scalar(first_key[:, 2:3], first_key[:, 1:2], 8.0, 16.0, ALU.add, ALU.min))
                for v in range(3):
                    chain(nc.vector.tensor_scalar(key_ge[:, :], key_col[:, :], first_key[:, v:v + 1], None, ALU.is_ge))
                    chain(nc.vector.tensor_scalar(first_key[:, 3:4], first_key[:, v:v + 1], float(NB), None, ALU.add))
                    chain(nc.vector.scalar_tensor_tensor(out=mask[:, v, :], in0=key_col[:, :], scalar=first_key[:, 3:4],
                                                              in1=key_ge[:, :], op0=ALU.is_lt, op1=ALU.mult))
                    chain(nc.vector.tensor_scalar(mask[:, v, :], mask[:, v, :], -1.0, 1e30, ALU.add, ALU.mult))
                chain(nc.vector.tensor_scalar(inv_n[:, :], key_col[:, 0:NB * GRID_R:GRID_R], 1.0, None, ALU.add))
                nc.vector.reciprocal(inv_n[:, :], inv_n[:, :]).then_inc(mask_done, 1)
                dve.wait_ge(mask_done, 1)

            def pool_group(g):
                w = WINDOWS[g]
                u = pT[:, g, :]
                if g >= 1:
                    dve.wait_ge(pooled_done, g)
                chain(nc.vector.tensor_tensor(window[:, 0, 1:PADW], u[:, 0:PADW - 1], u[:, 1:PADW], ALU.add))
                reach, cur, lo, hi = 1, 0, 1, PADW
                while 2 * reach < w:
                    a, b = lo + reach, hi - reach
                    chain(nc.vector.tensor_tensor(window[:, 1 - cur, a:b], window[:, cur, a - reach:b - reach],
                                                       window[:, cur, a + reach:b + reach], ALU.add))
                    lo, hi, reach, cur = a, b, 2 * reach, 1 - cur
                half = w // 2
                for at_, length in ((PAD_X, SEQ), (PAD_C, CTX)):
                    left = window[:, cur, at_:at_ + half]
                    chain(nc.vector.scalar_tensor_tensor(out=left, in0=left, scalar=float(w), in1=inv_n[:, half - 1:w - 1],
                                                              op0=ALU.mult, op1=ALU.mult))
                    if half > 1:
                        right = window[:, cur, at_ + length - half + 1:at_ + length]
                        chain(nc.vector.scalar_tensor_tensor(out=right, in0=right, scalar=float(w),
                                                                  in1=inv_n[:, half:w - 1][:, ::-1],
                                                                  op0=ALU.mult, op1=ALU.mult))
                nc.vector.scalar_tensor_tensor(out=u[:, PAD_X:PAD_C + CTX], in0=window[:, cur, PAD_X:PAD_C + CTX],
                                               scalar=1.0 / w, in1=u[:, PAD_X:PAD_C + CTX], op0=ALU.mult,
                                               op1=ALU.subtract).then_inc(pooled_done, 1)

            for j in range(16):
                project(j)
                if j == 4:
                    masks()
                if 5 <= j < 5 + KP:
                    pool_group(j - 5)
            for g in range(KP):
                dve.wait_ge(mixed_hi, g + 1)
                nc.vector.tensor_tensor(hl[:, g, :], att_f[:, g % 2, :], hh[:, g, :].bitcast(F32), ALU.subtract)\
                    .then_inc(mixed_split, 1)

            def normalise(s):
                h, j = STEPS[s]
                W = NK + CTX if j < BLOCKS else CTX
                b = s % 2
                dve.wait_ge(prob_done, s + 1)
                chain(nc.vector.reciprocal(rowinv[:, b:b + 1], rowsum[:, b:b + 1]))
                nc.vector.tensor_scalar(prob[:, b, 0:W], prob[:, b, 0:W], rowinv[:, b:b + 1], None, ALU.mult)\
                    .then_inc(prob_scaled, 1)

            def take_heads(t):
                dve.wait_ge(pv_done, (2 * t + 2) * (BLOCKS + 2))
                f = att_f[:, t % 2, :]
                o, oc = pC[:, (t % 2) * 512:(t % 2) * 512 + SEQ], pR[:, (t % 2) * 512:(t % 2) * 512 + CTX]
                nc.vector.tensor_copy(f[:, 0:SEQ].rearrange("p (r c) -> p r c", c=GRID_W),
                                      o[:, ::-1].rearrange("p (c r) -> p r c", r=GRID_R))
                chain(nc.vector.tensor_copy(f[:, SEQ:T], oc))
                chain(nc.vector.tensor_copy(hh[:, KP + t, :], f))
                nc.vector.tensor_tensor(hl[:, KP + t, :], f, hh[:, KP + t, :].bitcast(F32), ALU.subtract)\
                    .then_inc(mixed_split, 1)

            for s, (h, j) in enumerate(STEPS):
                W = NK + CTX if j < BLOCKS else CTX
                b = s % 2
                dve.wait_ge(scores_done, s + 1)
                nc.vector.reduce_max(rowmax[:, b:b + 1], pA[:, b * 512:b * 512 + W], AX_X, negate=True)\
                    .then_inc(max_done, 1)
                if s >= 1:
                    normalise(s - 1)
                if j == 3 and h % 2 == 0 and h >= 2:
                    take_heads(h // 2 - 1)
            normalise(len(STEPS) - 1)
            take_heads(3)
            outputs("about", P_ABOUT)
            norm("about")
            ffn(1)
            ffn(2)

            dve.wait_ge(panel_used, P_RG + 1)
            nc.vector.memset(upad[:, :], 0.0).then_inc(rg_ready, 1)
            for d in range(2):
                nc.vector.memset(gate_r[d][:, :], 0.0)
                last = nc.vector.memset(gate_i[d][:, :], 0.0)
            last.then_inc(rg_ready, 1)

            def convolve(n, between=None):
                dve.wait_ge(u_done, n + 1)
                if n >= 1:
                    dve.wait_ge(conv_split, n)
                cw = [cols[:, R_CONVW + k * KR + n:R_CONVW + k * KR + n + 1] for k in range(CONV)]
                cb = cols[:, R_CONVB + n:R_CONVB + n + 1]
                a = PAD_X - CONV // 2
                chain(nc.vector.tensor_scalar(conv[n % 2][:, :], upad[:, a:a + TG], cw[0], cb, ALU.mult, ALU.add))
                for k in range(1, CONV):
                    ins = nc.vector.scalar_tensor_tensor(out=conv[n % 2][:, :], in0=upad[:, a + k:a + k + TG], scalar=cw[k],
                                                         in1=conv[n % 2][:, :], op0=ALU.mult, op1=ALU.add)
                    if k < CONV - 1:
                        chain(ins)
                    if k == 1 and between is not None:
                        between()
                ins.then_inc(conv_done, 1)
                dve.wait_ge(conv_done, n + 1)
                if n >= 2:
                    dve.wait_ge(panel_used, gate_panel(n - 2) + 1)
                nc.vector.tensor_copy(ch[n % 2][:, :], conv[n % 2][:, :]).then_inc(conv_hi, 1)

            def gelu_inner(n):
                dve.wait_ge(gelu_q, n + 1)
                nc.vector.scalar_tensor_tensor(out=gel_z[:, :], in0=gel_q[:, :], scalar=1.0, in1=pB[:, 0:SEQ],
                                               op0=ALU.add, op1=ALU.mult).then_inc(gelu_z, 1)

            def gelu_outer(n):
                dve.wait_ge(gelu_t, n + 1)
                nc.vector.scalar_tensor_tensor(out=gel[:, n % 2, :], in0=gel_q[:, :], scalar=1.0, in1=pB[:, 0:SEQ],
                                               op0=ALU.add, op1=ALU.mult).then_inc(gelu_done, 1)

            def recur(n):
                for d in range(2):
                    dve.wait_ge(gates_done, 4 * n + 3 + d)
                    chain(nc.vector.scalar_tensor_tensor(out=gate_i[d][:, :], in0=gate_i[d][:, :], scalar=1.0,
                                                              in1=conv[n % 2][:, :], op0=ALU.add, op1=ALU.mult))
                for d in range(2):
                    a, b = decay[d], gate_i[d]
                    dve.wait_ge(root_done, 2 * n + d + 1)
                    chain(nc.vector.scalar_tensor_tensor(out=root[d][:, :], in0=a[:, :], scalar=1.0,
                                                              in1=root[d][:, :], op0=ALU.add, op1=ALU.mult))
                    chain(nc.vector.tensor_tensor(b[:, :], b[:, :], root[d][:, :], ALU.mult))
                    step, end = (1, TG - 1) if d == 0 else (-1, GAP_C)
                    ac, bc = a[:, GAP_C:TG][:, ::step], b[:, GAP_C:TG][:, ::step]
                    chain(nc.vector.tensor_tensor_scan(ac, ac, bc, 0.0, ALU.mult, ALU.add))
                    ax, bx = a[:, 0:SEQ][:, ::step], b[:, 0:SEQ][:, ::step]
                    nc.vector.tensor_tensor_scan(ax, ax, bx, a[:, end:end + 1], ALU.mult, ALU.add).then_inc(scan_done, 1)
                dve.wait_ge(scan_done, 2 * n + 2)
                chain(nc.vector.tensor_tensor(decay[0][:, 0:SEQ], decay[0][:, 0:SEQ], decay[1][:, 0:SEQ], ALU.add))
                if n >= 1:
                    dve.wait_ge(y_split, n)
                dve.wait_ge(gelu_done, n + 1)
                nc.vector.scalar_tensor_tensor(out=yf[:, :], in0=gel[:, n % 2, :], scalar=0.5, in1=decay[0][:, 0:SEQ],
                                               op0=ALU.mult, op1=ALU.mult).then_inc(y_done, 1)
                dve.wait_ge(y_done, n + 1)
                nc.vector.tensor_copy(yh[:, n, :], yf[:, :]).then_inc(y_hi_done, 1)

            convolve(0)
            gelu_inner(0)
            for n in range(1, KR):
                convolve(n, lambda: gelu_outer(n - 1))
                recur(n - 1)
                gelu_inner(n)
            gelu_outer(KR - 1)
            recur(KR - 1)
            outputs("rgout", P_RGOUT)
            norm("rgout")
            ffn(3)

        @block.tensor
        def _(pe):
            def passes(dst, par, kk, hi, lo, start, stop):
                w1, w2 = wh[:, par, kk * P:(kk + 1) * P], wl[:, par, kk * P:(kk + 1) * P]
                nc.tensor.matmul(dst, w1, hi, start=start, stop=False)
                nc.tensor.matmul(dst, w1, lo, start=False, stop=False)
                return nc.tensor.matmul(dst, w2, hi, start=False, stop=stop)

            def k_tile(ps, par, k, kt, hi, lo, W):
                last = passes(ps[:, 0:SEQ], par, k, hi[:, k, 0:SEQ], lo[:, k, 0:SEQ], k == 0, k == kt - 1)
                if W == T:
                    last = passes(ps[:, 512:512 + CTX], par, k, hi[:, k, SEQ:T], lo[:, k, SEQ:T], k == 0, k == kt - 1)
                return last

            def panel(ps, par, kt, hi, lo, W, each=None):
                for k in range(kt):
                    if each:
                        each(k)
                    last = k_tile(ps, par, k, kt, hi, lo, W)
                last.then_inc(panel_used, 1)

            def first_panels(p, each, W0, W1):
                pe.wait_ge(split_ready, p + 2)
                for k in range(KD):
                    each(k)
                    last = k_tile(pA, 0, k, KD, hh, hl, W0)
                    if k == KD - 1:
                        last.then_inc(panel_used, 1)
                    if k % 2 == 1:
                        k_tile(pB, 1, k // 2, KD, hh, hl, W1)
                for k in range(KD // 2, KD):
                    last = k_tile(pB, 1, k, KD, hh, hl, W1)
                last.then_inc(panel_used, 1)

            def use_ada(q):
                pe.wait_ge(ada_summed, sums_before(q + 1))
                pe.wait_ge(mods_done, q - (ADA0 - 1))
                for t in range(2):
                    for v in range(2):
                        last = nc.tensor.matmul(pC[:, 2 * t + v:2 * t + v + 1], ada_sum[:, v, t * P:(t + 1) * P],
                                                ones[:, 0:1], start=True, stop=True)
                last.then_inc(ada_used, 1)

            def after_norm(name):
                i = NORM_AT[name]

                def each(k):
                    pe.wait_ge(h_ready, i * KD + k + 1)
                    if name not in X_ONLY:
                        pe.wait_ge(h_ctx_ready, i * KD + k + 1)

                return each

            def gate_up(f, h, each):
                W = SEQ if f == 3 else T
                p0, F0 = first[f"gu{f}{h}"], GU_BEFORE[f, h]
                q0 = ada_first.get(f"gu{f}{h}")
                if each is not None:
                    first_panels(p0, each, W, W)
                    if q0 is not None:
                        use_ada(q0)
                with pe.Fori(int(each is not None), KC) as i:
                    pe.wait_ge(split_ready, i * 2 + (p0 + 1))
                    pe.wait_ge(silu_done, i + (F0 + 1))
                    if h == 1:
                        pe.wait_ge(resid_done, UPD[f"dn{f}0"] + KD - 1)
                    panel(pA, 0, KD, hh, hl, W)
                    pe.wait_ge(split_ready, i * 2 + (p0 + 2))
                    pe.wait_ge(gate_up_done, i + (F0 + 1))
                    if h == 1:
                        pe.wait_ge(resid_done, UPD[f"dn{f}0"] + KD)
                    panel(pB, 1, KD, hh, hl, W)
                    if q0 is not None:
                        use_ada(i + q0)

            def outputs(name, p0, kt, hi, lo, start=0, each=None):
                W = SEQ if name in X_ONLY else T
                q0 = ada_first.get(name)
                with pe.Fori(start, KD // 2) as i:
                    for r in range(2):
                        pe.wait_ge(split_ready, i * 2 + (p0 + r + 1))
                        pe.wait_ge(resid_done, i * 2 + (UPD[name] + r - 1))
                        panel(pair[r], r, kt, hi, lo, W, each)
                        if q0 is not None and r == 0:
                            use_ada(i + q0)

            def norm(name):
                i = NORM_AT[name]
                W = SEQ if name in X_ONLY or name == "dn31" else T
                pe.wait_ge(sum_done, (i + 1) * (KD - 1))
                for t in range(W // P):
                    last = nc.tensor.matmul(pC[:, 512 + t:513 + t], acc[:, t * P:(t + 1) * P], ones[:, 0:1],
                                            start=True, stop=True)
                last.then_inc(ss_done, 1)
                for t in range(W // P):
                    pe.wait_ge(diag_done, norm_tiles_before(i) + t + 1)
                    nc.tensor.matmul(pR[:, t * P:(t + 1) * P], ones[:, :], acc[:, t * P:(t + 1) * P], start=True,
                                     stop=True).then_inc(rbc_done, 1)

            def last_tile(n):
                return lambda k: k == KC - 1 and pe.wait_ge(g_split_done, n)

            def ffn(f, after):
                for h in range(2):
                    gate_up(f, h, after_norm(after) if h == 0 else None)
                    pe.wait_ge(silu_done, GU_BEFORE[f, h] + KC + 1)
                    pe.wait_ge(g_split_done, GU_BEFORE[f, h] + KC)
                    outputs(f"dn{f}{h}", first[f"dn{f}{h}"], KC, gh, gl, 0, last_tile(GU_BEFORE[f, h] + KC + 1))
                norm(f"dn{f}1")

            pe.wait_ge(const_done, 3)
            pe.wait_ge(rows_landed, 16 * ROW_DMAS)
            for t in range(3):
                n = min(P, ROWS - t * P)
                last = nc.tensor.transpose(pR[:, t * P:t * P + n], rowbuf[0:n, t, :], ident[0:n, 0:n])
            last.then_inc(cols_t, 1)
            pe.wait_ge(x_landed, 32)
            for k in range(KD):
                if k >= 2:
                    pe.wait_ge(resid_done, k - 1)
                for t in range(T // P):
                    last = nc.tensor.transpose(pair[k % 2][:, t * P:(t + 1) * P], xin[:, t, k * P:(k + 1) * P],
                                               ident[:, :])
                last.then_inc(xt_done, 1)
            pe.wait_ge(silu_done, 1)
            for chunk in range(2):
                pe.wait_ge(ada0_landed[chunk], 16)
                for t in range(chunk * ADA0 // 2, (chunk + 1) * ADA0 // 2):
                    for k in range(KD):
                        nc.tensor.matmul(pC[:, 2 * t:2 * t + 2], ada0[:, k, t * P:(t + 1) * P], cvec[:, k, :],
                                         start=(k == 0), stop=(k == KD - 1))
                if chunk == 0:
                    norm("in")
            for t in range(ADA0, 2 * ADA0):
                half, j = divmod(t - ADA0, ADA0 // 2)
                pe.wait_ge(ada0_summed, 2 * KD * (half + 1))
                for v in range(2):
                    last = nc.tensor.matmul(pC[:, 2 * t + v:2 * t + v + 1], ada0_sum[:, half, v, j * P:(j + 1) * P],
                                            ones[:, 0:1], start=True, stop=True)
            last.then_inc(ada_used, 1)
            pe.wait_ge(cols_done, 1)
            ffn(0, "in")

            def turn_values(m):
                pe.wait_ge(v_rows_done, m + 1)
                if m >= 2:
                    pe.wait_ge(proj_done, 2 + KP + m - 1)
                ps = pC if m % 2 == 0 else pR
                for t in range(T // P):
                    last = nc.tensor.transpose(ps[:, t * P:(t + 1) * P], v_rows[:, t * P:(t + 1) * P], ident[:, :])
                last.then_inc(v_turned, 1)

            for n in range(4):
                if n == 1:
                    for m in range(KP):
                        pe.wait_ge(split_ready, P_AB + KP + m + 1)
                        if m < 2:
                            pe.wait_ge(proj_done, KP + m + 1)
                        else:
                            pe.wait_ge(v_rows_done, m - 1)
                        panel(pair[m % 2], m % 2, KD, hh, hl, T)
                        if m >= 1:
                            turn_values(m - 1)
                    turn_values(KP - 1)
                    continue
                if n == 0:
                    first_panels(P_AB, after_norm("dn01"), T, T)
                with pe.Fori(int(n == 0), 2) as i:
                    for r in range(2):
                        pe.wait_ge(split_ready, i * 2 + (P_AB + 4 * n + r + 1))
                        pe.wait_ge(proj_done, i * 2 + (4 * n + r + 1))
                        panel(pair[r], r, KD, hh, hl, T)
            pe.wait_ge(poolw_landed, 16)
            for g in range(KP):
                pe.wait_ge(pooled_done, g + 1)
                if g >= 2:
                    pe.wait_ge(mixed_done, g - 1)
                ps = pC if g % 2 == 0 else pR
                nc.tensor.matmul(ps[:, 0:SEQ], poolw[:, g, :], pT[:, g, PAD_X:PAD_X + SEQ], start=True, stop=True)
                nc.tensor.matmul(ps[:, 512:512 + CTX], poolw[:, g, :], pT[:, g, PAD_C:PAD_C + CTX], start=True,
                                 stop=True).then_inc(poolmm_done, 1)

            def scores(s):
                h, j = STEPS[s]
                t, a = divmod(h, 2)
                rows = slice(a * DH, (a + 1) * DH)
                b = s % 2
                if s >= 2:
                    pe.wait_ge(prob_done, s - 1)
                else:
                    pe.wait_ge(proj_done, 2 + 16)
                bank = pA[:, b * 512:(b + 1) * 512]
                if j < BLOCKS:
                    q = qT[rows, t, (BLOCKS - 1 - j) * P:(BLOCKS - j) * P]
                    if j == 0:
                        pe.wait_ge(bias_done, h + 1)
                    k0 = SLAB_AT[j] * GRID_R
                    nc.tensor.matmul(bank[:, 0:NK], q, kT[rows, t, k0:k0 + NK], start=True, stop=False)
                    nc.tensor.matmul(bank[:, 0:NK], ident[:, :], bias[:, h % 2, VARIANT[j], :], start=False, stop=True)
                    last = nc.tensor.matmul(bank[:, NK:NK + CTX], q, kT[rows, t, SEQ:T], start=True, stop=True)
                else:
                    q = qT[rows, t, j * P:(j + 1) * P]
                    last = nc.tensor.matmul(bank[:, 0:CTX], q, kT[rows, t, SEQ:T], start=True, stop=True)
                last.then_inc(scores_done, 1)

            def turn(s):
                h, j = STEPS[s]
                b = s % 2
                pe.wait_ge(prob_scaled, s + 1)
                if s >= 2:
                    pe.wait_ge(prob_t_done, s - 1)
                for t in range(4 if j < BLOCKS else 2):
                    last = nc.tensor.transpose(pB[:, b * 512 + t * P:b * 512 + (t + 1) * P], prob[:, b, t * P:(t + 1) * P],
                                               ident[:, :])
                last.then_inc(turned_done, 1)

            def values(s):
                h, j = STEPS[s]
                t, a = divmod(h, 2)
                rows = slice(a * DH, (a + 1) * DH)
                b = s % 2
                pe.wait_ge(prob_t_done, s + 1)
                if s == 0:
                    pe.wait_ge(v_loaded, 16 * BLOCKS)
                    pe.wait_ge(mixed_done, KP)
                if j == 0 and a == 0 and t >= 2:
                    pe.wait_ge(mixed_split, KP + t - 1)
                if j < BLOCKS:
                    c0 = (t % 2) * 512 + (BLOCKS - 1 - j) * P
                    dst = pC[rows, c0:c0 + P]
                    tiles = [vslab[:, 2 * j, h * DH:(h + 1) * DH], vslab[:, 2 * j + 1, h * DH:(h + 1) * DH]]
                else:
                    dst = pR[rows, (t % 2) * 512 + (j - BLOCKS) * P:(t % 2) * 512 + (j - BLOCKS + 1) * P]
                    tiles = []
                tiles += [vtok[:, SEQ // P + i, h * DH:(h + 1) * DH] for i in range(2)]
                for i, v in enumerate(tiles):
                    last = nc.tensor.matmul(dst, v, prob_t[:, b, i * P:(i + 1) * P], start=(i == 0),
                                            stop=(i == len(tiles) - 1))
                last.then_inc(pv_done, 1)

            n = len(STEPS)
            scores(0)
            for s in range(n):
                if s + 1 < n:
                    scores(s + 1)
                if s >= 1:
                    values(s - 1)
                turn(s)
            values(n - 1)
            pe.wait_ge(mixed_split, 2 * KP)
            outputs("about", P_ABOUT, KD, hh, hl)
            norm("about")
            ffn(1, "about")
            ffn(2, "dn11")

            def u_rows(p, par, n):
                pe.wait_ge(split_ready, p + 1)
                pe.wait_ge(u_done, n)
                panel(pA, par, KD, hh, hl, T)

            def g_rows(p, par, n):
                pe.wait_ge(split_ready, p + 1)
                pe.wait_ge(gelu_done, n)
                panel(pB, par, KD, hh, hl, SEQ)

            def gates(p, par, b, n, u_read=None):
                pe.wait_ge(split_ready, p + 1)
                pe.wait_ge(conv_split, n + 1)
                for d in range(2):
                    xr, xi = (pB[:, 512:1024], pC[:, 0:512]) if d == 0 else (pR[:, 0:512], pR[:, 512:1024])
                    cc = pC[:, 512:1024] if d == 0 else pA[:, 512:1024]
                    for g in range(2):
                        passes(xr if g == 0 else xi, par, 2 * d + g, ch[b][:, 0:SEQ], cl[b][:, 0:SEQ], True, True)
                    if d == 1 and u_read is not None:
                        pe.wait_ge(u_done, u_read)
                    for g in range(2):
                        last = passes(cc[:, g * CTX:(g + 1) * CTX], par, 2 * d + g, ch[b][:, GAP_C:TG],
                                      cl[b][:, GAP_C:TG], True, True)
                last.then_inc(panel_used, 1)

            first_panels(P_RG, after_norm("dn21"), T, SEQ)
            u_rows(P_RG + 2, 0, 1)
            gates(P_RG + 3, 1, 0, 0, 2)
            g_rows(P_RG + 4, 0, 1)
            with pe.Fori(0, KR // 2 - 1) as i:
                for b in range(2):
                    p = i * 6 + (P_RG + 5 + 3 * b)
                    pe.wait_ge(gates_done, i * 8 + 4 * (b + 1))
                    u_rows(p, 1 - b, i * 2 + (2 + b))
                    gates(p + 1, b, 1 - b, i * 2 + (1 + b), i * 2 + (3 + b))
                    g_rows(p + 2, 1 - b, i * 2 + (2 + b))
            pe.wait_ge(gates_done, 4 * (KR - 1))
            gates(P_RG + 3 * KR - 1, 1, (KR - 1) % 2, KR - 1)
            for r in range(2):
                pe.wait_ge(split_ready, P_RGOUT + r + 1)
                if r == 1:
                    pe.wait_ge(gelu_done, KR)
                for k in range(KR - 1):
                    if r == 0:
                        pe.wait_ge(y_split, k + 1)
                    passes(pair[r][:, 0:SEQ], r, k, yh[:, k, :], yl[:, k, :], k == 0, False)
            pe.wait_ge(y_split, KR)
            for r in range(2):
                k = KR - 1
                passes(pair[r][:, 0:SEQ], r, k, yh[:, k, :], yl[:, k, :], False, True).then_inc(panel_used, 1)
            outputs("rgout", P_RGOUT, KR, yh, yl, 1)
            norm("rgout")
            ffn(3, "rgout")
            for k in range(KD):
                pe.wait_ge(final_scaled, k + 1)
                if k >= 2:
                    pe.wait_ge(out_copied, k - 1)
                for t in range(SEQ // P):
                    last = nc.tensor.transpose(pair[k % 2][:, t * P:(t + 1) * P], gbuf[:, k % 2, t * P:(t + 1) * P],
                                               ident[:, :])
                last.then_inc(out_t, 1)


_INS = ['x', 'c', 'ctx', 'c_ctx', 'ada_w', 'ada_b', 'norm_g', 'ffn_w_gu', 'ffn_w_down', 'ab_w_in', 'ab_w_out', 'pool_w',
        'pool_scale', 'na_rpb', 'rg_w_in', 'rg_conv_w', 'rg_conv_b', 'rg_gate_w', 'rg_gate_b', 'rg_lambda', 'rg_w_out',
        'final_g']


def kernel(**inputs):
    import numpy as _np
    import concourse.bacc as _bacc
    from concourse.bass_utils import run_bass_kernel_spmd as _run

    nc = _bacc.Bacc("TRN2", target_bir_lowering=False, num_devices=1)
    arrays, args = {}, []
    for name in _INS:
        a = _np.ascontiguousarray(inputs[name])
        arrays[f"in_{name}_dram"] = a
        args.append(nc.dram_tensor(f"in_{name}_dram", a.shape, F32, kind="ExternalInput").ap())
    args.append(nc.dram_tensor("rpb_padded_dram", (1, 32 + HEADS * RPB_R * RPB_C), F32, kind="Internal").ap())
    args.append(nc.dram_tensor("rpb_opened_dram", (HEADS, P, TABLE), F32, kind="Internal").ap())
    args.append(nc.dram_tensor("v_columns_dram", (SEQ, KP * P), F32, kind="Internal").ap())
    args.append(nc.dram_tensor("out_0_dram", (1, SEQ, D), F32, kind="ExternalOutput").ap())
    trunk(nc, *args)
    r = _run(nc, [arrays], core_ids=[0])
    return r.results[0]["out_0_dram"]
```
